# Optimizing a Trainium2 kernel written in Bass

```python
import jax, jax.numpy as jnp
from jax import lax
import numpy as np

D_MODEL = 2048
BATCH = 1
SEQ = 256
DEPTH = 1

EPS = 1e-6
CONV_A_WIDTH = D_MODEL
CONV_A_K = 3
SSM_EXPAND = 2
SSM_D_INNER = SSM_EXPAND * D_MODEL
SSM_HEAD_DIM = 64
SSM_HEADS = SSM_D_INNER // SSM_HEAD_DIM
SSM_GROUPS = 8
SSM_STATE = 128
SSM_CONV_K = 4
SSM_CONV_DIM = SSM_D_INNER + 2 * SSM_GROUPS * SSM_STATE
SSM_CHUNK = 128
SSM_NORM_GROUP = SSM_D_INNER // SSM_GROUPS
D_FF = -(-(8 * D_MODEL) // (3 * 256)) * 256

OFF_GATE_A = 0
OFF_GATE_B = D_MODEL
OFF_A = 2 * D_MODEL
OFF_Z = OFF_A + 3 * CONV_A_WIDTH
OFF_XBC = OFF_Z + SSM_D_INNER
OFF_DT = OFF_XBC + SSM_CONV_DIM
IN_COLS = OFF_DT + SSM_HEADS

kernel_name = "hybrid_shortconv_ssd_gated_block"

def rms_norm(x, g):
    xf = x.astype(jnp.float32)
    y = xf * lax.rsqrt(jnp.mean(xf * xf, axis=-1, keepdims=True) + EPS)
    return (y * g.astype(jnp.float32)).astype(x.dtype)

def causal_depthwise_conv(u, w):
    k = w.shape[0]
    t = u.shape[1]
    up = jnp.pad(u, ((0, 0), (k - 1, 0), (0, 0)))
    out = up[:, 0:t] * w[0]
    for j in range(1, k):
        out = out + up[:, j:j + t] * w[j]
    return out

def short_gated_conv_mixer(u_a, conv_w, w_out):
    b_gate, c_gate, h = jnp.split(u_a, 3, axis=-1)
    y = b_gate * causal_depthwise_conv(c_gate * h, conv_w)
    return y @ w_out

def ssd_chunked(xs, dt, a, b_ssm, c_ssm):
    bsz, t, h, p = xs.shape
    g, n = b_ssm.shape[2], b_ssm.shape[3]
    r = h // g
    q = SSM_CHUNK
    nc = t // q
    x_c = xs.reshape(bsz, nc, q, g, r, p)
    dt_c = dt.reshape(bsz, nc, q, g, r)
    b_c = b_ssm.reshape(bsz, nc, q, g, n)
    c_c = c_ssm.reshape(bsz, nc, q, g, n)
    xdt = x_c * dt_c[..., None]
    log_a = (dt_c * a.reshape(g, r)).transpose(0, 1, 3, 4, 2)
    cs = jnp.cumsum(log_a, axis=-1)
    causal = jnp.tril(jnp.ones((q, q), dtype=bool))
    seg = jnp.where(causal, cs[..., :, None] - cs[..., None, :], -jnp.inf)
    decay_in = jnp.exp(seg)
    cb = jnp.einsum('bclgn,bcsgn->bcgls', c_c, b_c)
    y_diag = jnp.einsum('bcgrls,bcsgrp->bclgrp', cb[:, :, :, None] * decay_in, xdt)
    decay_to_end = jnp.exp(cs[..., -1:] - cs)
    chunk_states = jnp.einsum('bclgn,bcgrl,bclgrp->bcgrpn', b_c, decay_to_end, xdt)
    chunk_decay = jnp.exp(cs[..., -1])

    def step(state, inp):
        s_new, dec = inp
        return dec[..., None, None] * state + s_new, state

    states_t = jnp.moveaxis(chunk_states, 1, 0)
    decay_t = jnp.moveaxis(chunk_decay, 1, 0)
    _, prev = lax.scan(step, jnp.zeros_like(states_t[0]), (states_t, decay_t))
    prev_states = jnp.moveaxis(prev, 0, 1)
    y_off = jnp.einsum('bclgn,bcgrpn,bcgrl->bclgrp', c_c, prev_states, jnp.exp(cs))
    return (y_diag + y_off).reshape(bsz, t, h, p)

def mamba2_mixer(z, xbc, dt_raw, conv_w, conv_b, dt_bias, a_log, d_skip, norm_g, w_out):
    bsz, t, _ = z.shape
    xbc = jax.nn.silu(causal_depthwise_conv(xbc, conv_w) + conv_b)
    xs = xbc[..., :SSM_D_INNER].reshape(bsz, t, SSM_HEADS, SSM_HEAD_DIM)
    b_ssm = xbc[..., SSM_D_INNER:SSM_D_INNER + SSM_GROUPS * SSM_STATE].reshape(bsz, t, SSM_GROUPS, SSM_STATE)
    c_ssm = xbc[..., SSM_D_INNER + SSM_GROUPS * SSM_STATE:].reshape(bsz, t, SSM_GROUPS, SSM_STATE)
    dt = jax.nn.softplus(dt_raw.astype(jnp.float32) + dt_bias.astype(jnp.float32))
    a = -jnp.exp(a_log.astype(jnp.float32))
    y = ssd_chunked(xs, dt, a, b_ssm, c_ssm)
    y = y + d_skip.astype(jnp.float32)[:, None] * xs
    yz = (y.reshape(bsz, t, SSM_D_INNER) * jax.nn.silu(z.astype(jnp.float32)))
    yz = yz.reshape(bsz, t, SSM_GROUPS, SSM_NORM_GROUP)
    yz = yz * lax.rsqrt(jnp.mean(yz * yz, axis=-1, keepdims=True) + EPS)
    yz = yz.reshape(bsz, t, SSM_D_INNER) * norm_g.astype(jnp.float32)
    return yz.astype(z.dtype) @ w_out

def swiglu(u, w_gate, w_up, w_down):
    return (jax.nn.silu(u @ w_gate) * (u @ w_up)) @ w_down

def setup_inputs(seed: int = 0) -> dict:
    key = jax.random.key(seed)
    ks = jax.random.split(key, 20)
    L, D = DEPTH, D_MODEL
    f32 = jnp.float32

    def nrm(k, shape, fan_in):
        return jax.random.normal(k, shape, f32) * (fan_in ** -0.5)

    def gain(k, shape):
        return 1.0 + 0.02 * jax.random.normal(k, shape, f32)

    dt0 = jnp.exp(jax.random.uniform(ks[7], (L, SSM_HEADS), f32) * (np.log(0.1) - np.log(0.001)) + np.log(0.001))
    dt_bias = dt0 + jnp.log(-jnp.expm1(-dt0))
    a_log = jnp.log(jax.random.uniform(ks[8], (L, SSM_HEADS), f32, 1.0, 16.0))
    return {
        "x": jax.random.normal(ks[0], (BATCH, SEQ, D), f32),
        "norm_mix_g": gain(ks[1], (L, D)),
        "w_in": nrm(ks[2], (L, D, IN_COLS), D),
        "conv_a_w": nrm(ks[3], (L, CONV_A_K, CONV_A_WIDTH), CONV_A_K),
        "w_out_a": nrm(ks[4], (L, CONV_A_WIDTH, D), CONV_A_WIDTH),
        "ssm_conv_w": nrm(ks[5], (L, SSM_CONV_K, SSM_CONV_DIM), SSM_CONV_K),
        "ssm_conv_b": 0.02 * jax.random.normal(ks[6], (L, SSM_CONV_DIM), f32),
        "dt_bias": dt_bias,
        "a_log": a_log,
        "d_skip": gain(ks[9], (L, SSM_HEADS)),
        "ssm_norm_g": gain(ks[10], (L, SSM_D_INNER)),
        "w_out_ssm": nrm(ks[11], (L, SSM_D_INNER, D), SSM_D_INNER),
        "w_o": nrm(ks[12], (L, D, D), D),
        "norm_ffn_g": gain(ks[13], (L, D)),
        "w_ffn_gate": nrm(ks[14], (L, D, D_FF), D),
        "w_ffn_up": nrm(ks[15], (L, D, D_FF), D),
        "w_ffn_down": nrm(ks[16], (L, D_FF, D), D_FF),
        "norm_final_g": gain(ks[17], (D,)),
    }

def reference(x, norm_mix_g, w_in, conv_a_w, w_out_a, ssm_conv_w, ssm_conv_b, dt_bias, a_log,
              d_skip, ssm_norm_g, w_out_ssm, w_o, norm_ffn_g, w_ffn_gate, w_ffn_up, w_ffn_down,
              norm_final_g):
    h = x
    for i in range(DEPTH):
        u = rms_norm(h, norm_mix_g[i])
        proj = u @ w_in[i]
        gate_a = jax.nn.sigmoid(proj[..., OFF_GATE_A:OFF_GATE_B])
        gate_b = jax.nn.sigmoid(proj[..., OFF_GATE_B:OFF_A])
        y_a = short_gated_conv_mixer(proj[..., OFF_A:OFF_Z], conv_a_w[i], w_out_a[i])
        y_b = mamba2_mixer(proj[..., OFF_Z:OFF_XBC], proj[..., OFF_XBC:OFF_DT], proj[..., OFF_DT:IN_COLS],
                           ssm_conv_w[i], ssm_conv_b[i], dt_bias[i], a_log[i], d_skip[i],
                           ssm_norm_g[i], w_out_ssm[i])
        h = h + (gate_a * y_a + gate_b * y_b) @ w_o[i]
        h = h + swiglu(rms_norm(h, norm_ffn_g[i]), w_ffn_gate[i], w_ffn_up[i], w_ffn_down[i])
    return rms_norm(h, norm_final_g)


_drawn_inputs = setup_inputs


def setup_inputs(seed=0):
    import zlib

    import numpy as np

    out = dict(_drawn_inputs(seed))
    spreads = {}
    factors = {'ssm_conv_b': 4.327,
     'd_skip': 7.763,
     'ssm_norm_g': 5.948,
     'norm_ffn_g': 4.508,
     'norm_final_g': 2.825}
    for name, (base, spread) in spreads.items():
        noise = np.random.default_rng([zlib.crc32(name.encode()), seed]).standard_normal(out[name].shape)
        drawn = base * np.exp(spread * noise) if base else spread * noise
        out[name] = __import__('jax').numpy.asarray(drawn.astype(out[name].dtype))
    for name, factor in factors.items():
        out[name] = (out[name] * factor).astype(out[name].dtype)
    return out
```

```python
import concourse.bass as bass
from concourse import mybir
from contextlib import ExitStack
import numpy as np

FP32 = mybir.dt.float32
FP32R = mybir.dt.float32r
ALU = mybir.AluOpType
ACT = mybir.ActivationFunctionType

P = 128
D_MODEL = 2048
SEQ = 256
EPS = 1e-6
D_INNER = 2 * D_MODEL
HEAD_DIM = 64
HEADS = D_INNER // HEAD_DIM
GROUPS = 8
HEADS_G = HEADS // GROUPS
STATE = 128
CONV_DIM = D_INNER + 2 * GROUPS * STATE
CONV_K = 4
CONV_A_K = 3
D_FF = -(-(8 * D_MODEL) // (3 * 256)) * 256
OFF_GATE_A = 0
OFF_GATE_B = D_MODEL
OFF_A = 2 * D_MODEL
OFF_Z = OFF_A + 3 * D_MODEL
OFF_XBC = OFF_Z + D_INNER
OFF_DT = OFF_XBC + CONV_DIM

COLS = 512
TILES = COLS // P
KP = 2
SLOTS = 4
CHUNKS = SEQ // P
KD = D_MODEL // P
KF = D_FF // P
NP_D = KD // KP
NP_I = 2 * KD // KP
NP_F = KF // KP
BLK_D = D_MODEL // COLS
BLK_F = D_FF // COLS

CONV_TILES = CONV_DIM // P
PC_CONV_W = 0
PC_CONV_B = PC_CONV_W + CONV_K * CONV_TILES
PC_MIX_G = PC_CONV_B + CONV_TILES
PC_CONV_A = PC_MIX_G + KD
PC_SSM_G = PC_CONV_A + CONV_A_K * KD
PC_FFN_G = PC_SSM_G + 2 * KD
PC_ALL = PC_FFN_G + KD
PC_TABLES = -(-PC_ALL // P)

N_BC = 0
N_G = N_BC + 4 * NP_D
N_OS = N_G + GROUPS * 2 * NP_D
N_A = N_OS + BLK_D * (NP_D + NP_I)
N_OA = N_A + BLK_D * 3 * NP_D
N_O = N_OA + BLK_D * 2 * NP_D
N_F = N_O + BLK_D * NP_D
N_DN = N_F + BLK_F * 2 * NP_D
N_END = N_DN + BLK_D * NP_F


def hybrid_block_kernel(nc, x, norm_mix_g, w_in, conv_a_w, w_out_a, ssm_conv_w, ssm_conv_b, dt_bias,
                        a_log, d_skip, ssm_norm_g, w_out_ssm, w_o, norm_ffn_g, w_ffn_gate, w_ffn_up,
                        w_ffn_down, norm_final_g, out):
    ctx = ExitStack()
    with ctx:
        KIB = 1024
        BASE = -(-nc.sbuf_base // 64) * 64
        assert BASE + 207 * KIB + 512 <= nc.sbuf_usable_end

        def at(name, kib, shape, dt=FP32):
            return nc.alloc_sbuf_tensor_at(name, shape, dt, offset=BASE + int(kib * KIB))

        raw = [at(f"weights_raw{s}", 4 * s, [P, KP, COLS]) for s in range(SLOTS)]
        w_hi = [at(f"weights_hi{s}", 16 + 4 * s, [P, KP, COLS], FP32R) for s in range(SLOTS)]
        w_lo = [at(f"weights_lo{s}", 32 + 4 * s, [P, KP, COLS], FP32R) for s in range(SLOTS)]
        normed = at("normed", 48, [P, KD, 2, SEQ], FP32R)
        Q, R, CO, W = 80, 168, 184, 189

        params = at("params", CO, [P, PC_ALL])
        ident = at("ident", CO + 1.5, [P, P])
        upto = at("upto", CO + 2, [P, P])
        after = at("after", CO + 2.5, [P, P], FP32R)
        after_f = at("after_f", CO + 3, [P, P])
        row_sum = at("row_sum", CO + 3.5, [P, CHUNKS])
        row_ms = at("row_ms", CO + 3.5 + 1 / 16, [P, CHUNKS])
        row_rms = at("row_rms", CO + 3.5 + 2 / 16, [P, CHUNKS])
        row_rstd = at("row_rstd", CO + 3.5 + 3 / 16, [P, CHUNKS])
        grp_sum = at("grp_sum", CO + 3.5 + 4 / 16, [P, CHUNKS])
        grp_ms = at("grp_ms", CO + 3.5 + 5 / 16, [P, CHUNKS])
        grp_rms = at("grp_rms", CO + 3.5 + 6 / 16, [P, CHUNKS])
        grp_rstd = at("grp_rstd", CO + 3.5 + 7 / 16, [P, CHUNKS])

        x_tok = at("x_tok", Q, [P, CHUNKS, D_MODEL])
        x_nrm = at("x_nrm", Q + 16, [P, CHUNKS, D_MODEL])
        par_rows = at("par_rows", Q + 32, [P, PC_TABLES, P])
        dtw_raw = at("dtw_raw", Q + 34, [P, KD, HEADS])
        dtw_hi = at("dtw_hi", Q + 38, [P, KD, HEADS], FP32R)
        dtw_lo = at("dtw_lo", Q + 42, [P, KD, HEADS], FP32R)
        dt_tmp = [at(f"dt_tmp{j}", Q + 46 + j / 2, [P, CHUNKS * HEADS]) for j in range(10)]
        bias_b = at("bias_b", Q + 52, [P, HEADS])
        alog_b = at("alog_b", Q + 52.25, [P, HEADS])
        anow_b = at("anow_b", Q + 52.5, [P, HEADS])
        loga = at("loga", Q + 53, [P, CHUNKS, HEADS])

        yz = at("yz", Q, [P, 2 * KD, 2, SEQ], FP32R)
        b_feat = at("b_feat", Q + 56, [P, TILES, SEQ])
        c_feat = at("c_feat", Q + 60, [P, TILES, SEQ])
        S = Q + 64
        cb = at("cb", S, [P, GROUPS, CHUNKS, P])
        c_last = at("c_last", S + 8, [P, GROUPS, P])
        b_first = at("b_first", S + 12, [P, GROUPS, STATE])
        x_pre = at("x_pre", S + 16, [P, TILES, SEQ + CONV_K])
        x_conv = at("x_conv", S + 20.25, [P, TILES, SEQ])
        xdt = at("xdt", S + 24.25, [P, CHUNKS, COLS])
        y = at("y", S + 28.25, [P, CHUNKS, COLS])
        xdec = at("xdec", S + 32.25, [P, COLS])
        state_sb = at("state_sb", S + 34.25, [P, COLS])
        dt = at("dt", S + 36.25, [P, CHUNKS, HEADS])
        loga_hi = at("loga_hi", S + 36.75, [P, CHUNKS, HEADS], FP32R)
        loga_lo = at("loga_lo", S + 37.25, [P, CHUNKS, HEADS], FP32R)
        dec_end = at("dec_end", S + 37.75, [P, HEADS])
        dec_in = at("dec_in", S + 38, [P, HEADS])
        skip_b = at("skip_b", S + 38.25, [P, HEADS])
        b_now = at("b_now", S + 38.5, [P, STATE])
        c_now = at("c_now", S + 39, [P, P])
        seg_hi = at("seg_hi", W, [P, 4, P], FP32R)
        seg_lo = at("seg_lo", W + 2, [P, 4, P], FP32R)
        mix = at("mix", W + 4, [P, 4, 4, P])
        z_act = at("z_act", W + 12, [P, CHUNKS, COLS])

        gate_val = at("gate_val", W, [P, TILES, SEQ])
        val = at("val", W + 4, [P, TILES, SEQ])
        merged_b = at("merged_b", R, [P, KD, SEQ])
        ya = at("ya", Q, [P, KD, 2, SEQ], FP32R)
        merged = at("merged", Q + 32, [P, KD, 2, SEQ], FP32R)
        a_pre = at("a_pre", Q + 64, [P, TILES, SEQ + CONV_A_K])
        a_conv = at("a_conv", Q + 68.5, [P, TILES, SEQ])
        a_c = at("a_c", Q + 72.5, [P, TILES, SEQ])
        h_tok = at("h_tok", R, [P, CHUNKS, D_MODEL])
        x_res = at("x_res", Q, [P, CHUNKS, D_MODEL])
        h_nrm = at("h_nrm", Q + 16, [P, CHUNKS, D_MODEL])
        ff = at("ff", Q, [P, KF, 2, SEQ], FP32R)
        final_b = at("final_b", 48, [P, D_MODEL])
        y_out = at("y_out", 56, [P, CHUNKS, D_MODEL])

        ps = ctx.enter_context(nc.psum_tensor("ps", [P, 8, 512], FP32))

        def sem(name):
            return ctx.enter_context(nc.semaphore(name))

        weights_landed = [sem(f"weights_landed{s}") for s in range(SLOTS)]
        weights_hi, weights_split, weights_used = sem("weights_hi"), sem("weights_split"), sem("weights_used")
        x_landed, x2_landed = sem("x_landed"), sem("x2_landed")
        rows_landed, heads_landed, dtw_landed = sem("rows_landed"), sem("heads_landed"), sem("dtw_landed")
        final_landed, out_stored = sem("final_landed"), sem("out_stored")
        masks_set, masks_ready, after_ready, pads_zero = sem("masks_set"), sem("masks_ready"), sem("after_ready"), sem("pads_zero")
        params_t, params_ready = sem("params_t"), sem("params_ready")
        nrm_sum, nrm_ms, nrm_rms, nrm_rstd = sem("nrm_sum"), sem("nrm_ms"), sem("nrm_rms"), sem("nrm_rstd")
        nrm_scaled, nrm_t, nrm_hi, nrm_lo = sem("nrm_scaled"), sem("nrm_t"), sem("nrm_hi"), sem("nrm_lo")
        dtw_hi_ok, dtw_ready, dt_raw = sem("dtw_hi_ok"), sem("dtw_ready"), sem("dt_raw")
        dt_step, dt_exp, heads_exp = sem("dt_step"), sem("dt_exp"), sem("heads_exp")
        cs_ready, decays_ready = sem("cs_ready"), sem("decays_ready")
        acc_copied = sem("acc_copied")
        conv_first, conv_taps, conv_act = sem("conv_first"), sem("conv_taps"), sem("conv_act")
        b_t, b_kept, c_kept, cb_ready, cb_kept = sem("b_t"), sem("b_kept"), sem("c_kept"), sem("cb_ready"), sem("cb_kept")
        now_kept = sem("now_kept")
        z_kept, x_t, xprep = sem("z_kept"), sem("x_t"), sem("xprep")
        seg_in, seg_ready, seg_exp, mix_ready = sem("seg_in"), sem("seg_ready"), sem("seg_exp"), sem("mix_ready")
        y_first, y_second, state_kept, y_sum = sem("y_first"), sem("y_second"), sem("state_kept"), sem("y_sum")
        g_sq, g_ms, g_rms, g_scaled = sem("g_sq"), sem("g_ms"), sem("g_rms"), sem("g_scaled")
        yz_t, yz_hi, yz_lo = sem("yz_t"), sem("yz_hi"), sem("yz_lo")
        g_rstd = sem("g_rstd")
        gate_done, mb_done = sem("gate_done"), sem("mb_done")
        ac_kept, ch_done, a_first, a_taps = sem("ac_kept"), sem("ch_done"), sem("a_first"), sem("a_taps")
        val_part, val_done, out_hi, out_lo = sem("val_part"), sem("val_done"), sem("out_hi"), sem("out_lo")
        o_summed, d_summed, fin_ready = sem("o_summed"), sem("d_summed"), sem("fin_ready")

        block = ctx.enter_context(nc.Block())

        def blk2(b):
            return ps[:, b:b + 2, :].rearrange("p b (m t) -> p (b m) t", t=SEQ)

        def per_head(ap):
            return ap.unsqueeze(2).to_broadcast([P, HEADS_G, HEAD_DIM])

        def heads_of(ap):
            return ap.rearrange("p (h d) -> p h d", d=HEAD_DIM)

        rows = [ssm_conv_w.rearrange("a k (t p) -> (a k t) p", p=P),
                ssm_conv_b.rearrange("a (t p) -> (a t) p", p=P),
                norm_mix_g.rearrange("a (t p) -> (a t) p", p=P),
                conv_a_w.rearrange("a k (t p) -> (a k t) p", p=P),
                ssm_norm_g.rearrange("a (t p) -> (a t) p", p=P),
                norm_ffn_g.rearrange("a (t p) -> (a t) p", p=P)]
        parameter_loads, at_row = [], 0
        for r in rows:
            done = 0
            while done < r.shape[0]:
                n = min(r.shape[0] - done, P - at_row % P)
                parameter_loads.append((par_rows[at_row % P:at_row % P + n, at_row // P, :], r[done:done + n, :]))
                done += n
                at_row += n

        @block.sync
        def _(sp):
            def load(n, c, w, row0, col):
                s = c % SLOTS
                sp.dma_start(raw[s][:, :, :],
                             w[row0:row0 + KP * P, bass.ds(col, COLS)].rearrange("(k p) n -> p k n", p=P))\
                  .then_inc(weights_landed[s], 16)

            def load_block(n0, w, pieces, col, row_first=0, first=False):
                for c in range(pieces):
                    if not (first and c < SLOTS):
                        sp.wait_ge(weights_split, n0 + c - (SLOTS - 1))
                    load(n0 + c, c, w, (row_first + c) * KP * P, col)

            x_v = x[0].rearrange("(c p) d -> p c d", p=P)
            for c in range(CHUNKS):
                sp.dma_start(x_tok[:, c, :], x_v[:, c, :]).then_inc(x_landed, 16)
            sp.dma_start(dtw_raw[:, :, :], w_in[0][:, OFF_DT:OFF_DT + HEADS].rearrange("(k p) n -> p k n", p=P))\
              .then_inc(dtw_landed, 16)
            for i in range(2):
                load_block(N_BC + 2 * i * NP_D, w_in[0], NP_D, OFF_XBC + D_INNER + i * COLS, first=(i == 0))
                load_block(N_BC + (2 * i + 1) * NP_D, w_in[0], NP_D,
                           OFF_XBC + D_INNER + GROUPS * STATE + i * COLS)
            with sp.Fori(0, GROUPS) as g:
                load_block(N_G + g * (2 * NP_D), w_in[0], NP_D, OFF_XBC + g * COLS)
                load_block(N_G + g * (2 * NP_D) + NP_D, w_in[0], NP_D, OFF_Z + g * COLS)
            with sp.Fori(1, BLK_D + 1) as i:
                n = (N_OS - (NP_D + NP_I)) + i * (NP_D + NP_I)
                load_block(n, w_in[0], NP_D, (OFF_GATE_B - COLS) + i * COLS)
                load_block(n + NP_D, w_out_ssm[0], NP_I, i * COLS - COLS)
            with sp.Fori(0, BLK_D) as i:
                for j, part in enumerate((1, 2, 0)):
                    load_block(N_A + i * (3 * NP_D) + j * NP_D, w_in[0], NP_D, OFF_A + part * D_MODEL + i * COLS)
            with sp.Fori(0, BLK_D) as i:
                load_block(N_OA + i * (2 * NP_D), w_in[0], NP_D, OFF_GATE_A + i * COLS)
                load_block(N_OA + i * (2 * NP_D) + NP_D, w_out_a[0], NP_D, i * COLS)
            for k in range(NP_D):
                for c in range(BLK_D):
                    n = N_O + k * BLK_D + c
                    sp.wait_ge(weights_split, n - (SLOTS - 1))
                    load(n, c, w_o[0], k * KP * P, c * COLS)
                if k == 0:
                    sp.wait_ge(weights_used, N_O)
                    for c in range(CHUNKS):
                        sp.dma_start(x_res[:, c, :], x_v[:, c, :]).then_inc(x2_landed, 16)
            with sp.Fori(0, BLK_F) as i:
                load_block(N_F + i * (2 * NP_D), w_ffn_gate[0], NP_D, i * COLS)
                load_block(N_F + i * (2 * NP_D) + NP_D, w_ffn_up[0], NP_D, i * COLS)
            sp.wait_ge(weights_used, N_DN)
            sp.dma_start(final_b[:, :], norm_final_g.partition_broadcast(P)).then_inc(final_landed, 16)
            with sp.Fori(0, BLK_D // 2) as i:
                for c in range(2 * NP_F):
                    sp.wait_ge(weights_split, N_DN + i * (2 * NP_F) + c - (SLOTS - 1))
                    load(None, c, w_ffn_down[0], (c % NP_F) * KP * P, (2 * i + c // NP_F) * COLS)
            out_v = out[0].rearrange("(c p) d -> p c d", p=P)
            for c in range(CHUNKS):
                sp.wait_ge(fin_ready, c + 1)
                sp.dma_start(out_v[:, c, :], y_out[:, c, :]).then_inc(out_stored, 16)
            sp.wait_ge(out_stored, 16 * CHUNKS)

        @block.gpsimd
        def _(pool):
            for dst, src in parameter_loads:
                pool.dma_start(dst, src).then_inc(rows_landed, 16)
            for dst, src in ((bias_b, dt_bias), (alog_b, a_log), (skip_b, d_skip)):
                pool.dma_start(dst[:, :], src[0].partition_broadcast(P)).then_inc(heads_landed, 16)
            nc.gpsimd.memset(ident[:, :], 0.0).then_inc(masks_set, 1)
            nc.gpsimd.memset(upto[:, :], 1.0).then_inc(masks_set, 1)
            nc.gpsimd.memset(after_f[:, :], 1.0).then_inc(masks_set, 1)
            nc.gpsimd.memset(x_pre[:, :, 0:CONV_K - 1], 0.0).then_inc(pads_zero, 1)
            pool.wait_ge(masks_set, 3)
            nc.gpsimd.affine_select(out=ident[:, :], in_=ident[:, :], compare_op=ALU.not_equal, fill=1.0,
                                    base=0, pattern=[[-1, P]], channel_multiplier=1).then_inc(masks_ready, 1)
            nc.gpsimd.affine_select(out=upto[:, :], in_=upto[:, :], compare_op=ALU.is_ge, fill=0.0,
                                    base=0, pattern=[[1, P]], channel_multiplier=-1).then_inc(masks_ready, 1)
            nc.gpsimd.affine_select(out=after_f[:, :], in_=after_f[:, :], compare_op=ALU.is_gt, fill=0.0,
                                    base=0, pattern=[[-1, P]], channel_multiplier=1).then_inc(masks_ready, 1)
            pool.wait_ge(weights_used, N_A)
            nc.gpsimd.memset(a_pre[:, :, 0:CONV_A_K - 1], 0.0).then_inc(pads_zero, 1)

        @block.scalar
        def _(act):
            def hi(n, c):
                s = c % SLOTS
                act.wait_ge(weights_landed[s], hi_count(n, c))
                if not (isinstance(n, int) and n < SLOTS):
                    act.wait_ge(weights_used, n - (SLOTS - 1))
                nc.scalar.activation(w_hi[s][:, :, :], raw[s][:, :, :], ACT.Copy).then_inc(weights_hi, 1)

            def hi_count(n, c):
                return (n - c % SLOTS) * (16 // SLOTS) + 16

            def stream(n0, pieces, steps):
                for c in range(pieces):
                    hi(n0 + c, c)
                    for f in steps.get(c, []):
                        f()

            def norm_stats(src, k):
                junk = x_nrm if k == 0 else (h_nrm if k == 1 else y_out)
                for c in range(CHUNKS):
                    if k == 0:
                        act.wait_ge(x_landed, 16 * CHUNKS)
                    elif k == 1:
                        act.wait_ge(o_summed, 8)
                    else:
                        act.wait_ge(d_summed, 8)
                    nc.scalar.activation(junk[:, c, :], src[:, c, :], ACT.Square,
                                         accum_out=row_sum[:, c:c + 1]).then_inc(nrm_sum, 1)
                act.wait_ge(nrm_ms, k + 1)
                nc.scalar.activation(row_rms[:, :], row_ms[:, :], ACT.Sqrt).then_inc(nrm_rms, 1)

            def norm_hi(k, gcol):
                for b in range(KD // 2):
                    act.wait_ge(nrm_t, k * KD // 2 + b + 1)
                    for j in range(2):
                        t = 2 * b + j
                        nc.scalar.activation(normed[:, t, 0, :], ps[:, b, j * SEQ:(j + 1) * SEQ], ACT.Copy,
                                             scale=params[:, gcol + t:gcol + t + 1]).then_inc(nrm_hi, 1)

            norm_stats(x_tok, 0)
            act.wait_ge(params_ready, 1)
            norm_hi(0, PC_MIX_G)
            act.wait_ge(dtw_landed, 16)
            nc.scalar.activation(dtw_hi[:, :, :], dtw_raw[:, :, :], ACT.Copy).then_inc(dtw_hi_ok, 1)
            act.wait_ge(heads_landed, 48)
            nc.scalar.activation(anow_b[:, :], alog_b[:, :], ACT.Exp).then_inc(heads_exp, 1)

            def dt_exponential():
                act.wait_ge(dt_step, 3)
                nc.scalar.activation(dt_tmp[3][:, :], dt_tmp[2][:, :], ACT.Exp).then_inc(dt_exp, 1)

            def decays():
                act.wait_ge(cs_ready, 1)
                nc.scalar.activation(dec_end[:, :], ps[:, 7, 0:HEADS], ACT.Exp).then_inc(decays_ready, 1)
                nc.scalar.activation(dec_in[:, :], ps[:, 7, HEADS:2 * HEADS], ACT.Exp).then_inc(decays_ready, 1)

            def copy_block(q, used, bank):
                def f():
                    act.wait_ge(weights_used, used)
                    if not (isinstance(q, int) and q == 0):
                        act.wait_ge(conv_taps, q * 12)
                    else:
                        act.wait_ge(pads_zero, 1)
                    nc.scalar.activation(x_pre[:, :, CONV_K - 1:CONV_K - 1 + SEQ], blk2(bank), ACT.Copy)\
                        .then_inc(acc_copied, 1)
                return f

            def conv_first_tap(q, tile):
                def f():
                    act.wait_ge(acc_copied, q + 1)
                    if not (isinstance(q, int) and q == 0):
                        act.wait_ge(conv_act, q)
                    if not isinstance(q, int):
                        act.wait_ge(x_t, 2 * (q - 4))
                    for m in range(TILES):
                        nc.scalar.activation(
                            x_conv[:, m, :], x_pre[:, m, CONV_K - 1:CONV_K - 1 + SEQ], ACT.Identity,
                            scale=params[:, bass.ds(tile + (PC_CONV_W + (CONV_K - 1) * CONV_TILES + m), 1)],
                            bias=params[:, bass.ds(tile + (PC_CONV_B + m), 1)]).then_inc(conv_first, 1)
                return f

            def conv_silu(q, dst):
                def f():
                    act.wait_ge(conv_taps, (q + 1) * 12)
                    if isinstance(q, int) and q in (2, 3):
                        act.wait_ge(cb_ready, 1)
                    nc.scalar.activation(dst[:, :, :], x_conv[:, :, :], ACT.Silu).then_inc(conv_act, 1)
                return f

            def keep_b(i):
                def f():
                    act.wait_ge(b_t, i + 1)
                    nc.scalar.activation(b_first[:, TILES * i:TILES * (i + 1), :].rearrange("p g n -> p (g n)"),
                                         ps[:, 6, :], ACT.Copy).then_inc(b_kept, 1)
                return f

            def keep_c(i):
                def f():
                    act.wait_ge(conv_act, 2 * i + 2)
                    nc.scalar.activation(c_last[:, TILES * i:TILES * (i + 1), :], c_feat[:, :, P:2 * P],
                                         ACT.Copy).then_inc(c_kept, 1)
                return f

            B_TILE, C_TILE = D_INNER // P, D_INNER // P + GROUPS

            def c_steps(i):
                n = N_BC + (2 * i + 2) * NP_D
                return {1: [keep_b(i), copy_block(2 * i + 1, n, 4)],
                        2: [conv_first_tap(2 * i + 1, C_TILE + TILES * i)],
                        5: [conv_silu(2 * i + 1, c_feat), keep_c(i)]}

            for i in range(2):
                n = N_BC + 2 * i * NP_D
                steps = {9: [copy_block(2 * i, n + NP_D, 0)],
                         10: [conv_first_tap(2 * i, B_TILE + TILES * i)],
                         13: [conv_silu(2 * i, b_feat)]}
                if i == 0:
                    steps |= {3: [dt_exponential], 7: [decays]}
                else:
                    steps |= c_steps(0)
                stream(n, 2 * NP_D, steps)

            def now(g):
                def f():
                    act.wait_ge(c_kept, 2)
                    act.wait_ge(b_kept, 2)
                    if not (isinstance(g, int) and g == 0):
                        act.wait_ge(y_second, g)
                    nc.scalar.activation(b_now[:, :], b_first[:, bass.ds(g, 1), :].rearrange("p a n -> p (a n)"),
                                         ACT.Copy).then_inc(now_kept, 1)
                    nc.scalar.activation(c_now[:, :], c_last[:, bass.ds(g, 1), :].rearrange("p a n -> p (a n)"),
                                         ACT.Copy).then_inc(now_kept, 1)
                return f

            def keep_z(g, used):
                def f():
                    act.wait_ge(weights_used, used)
                    if not (isinstance(g, int) and g == 0):
                        act.wait_ge(g_sq, 2 * g)
                    nc.scalar.activation(z_act[:, :, :], ps[:, 4:6, :], ACT.Silu).then_inc(z_kept, 1)
                return f

            def seg_exponential(g, b):
                def f():
                    act.wait_ge(seg_ready, 4 * g + b + 1)
                    if not (isinstance(g, int) and g == 0):
                        act.wait_ge(y_first if b < 2 else y_second, g)
                    nc.scalar.activation(mix[:, b, :, :].rearrange("p h l -> p (h l)"), ps[:, 2 + b % 2, :],
                                         ACT.Exp).then_inc(seg_exp, 1)
                return f

            def keep_state(g):
                def f():
                    act.wait_ge(y_first, g + 1)
                    if not (isinstance(g, int) and g == 0):
                        act.wait_ge(y_second, g)
                    nc.scalar.activation(state_sb[:, :], ps[:, 6, :], ACT.Copy).then_inc(state_kept, 1)
                return f

            def group_squares(g):
                def f():
                    for c in range(CHUNKS):
                        act.wait_ge(y_sum, 6 * g + 6)
                        nc.scalar.activation(z_act[:, c, :], y[:, c, :], ACT.Square,
                                             accum_out=grp_sum[:, c:c + 1]).then_inc(g_sq, 1)
                return f

            def group_root(g):
                def f():
                    act.wait_ge(g_ms, g + 1)
                    nc.scalar.activation(grp_rms[:, :], grp_ms[:, :], ACT.Sqrt).then_inc(g_rms, 1)
                return f

            def keep_yz_hi(g):
                def f():
                    for m in range(TILES):
                        act.wait_ge(yz_t, 2 * g + m // 2 + 1)
                        nc.scalar.activation(
                            yz[:, bass.ds(TILES * g + m, 1), 0, :].rearrange("p a t -> p (a t)"),
                            ps[:, 6 + m // 2, (m % 2) * SEQ:(m % 2 + 1) * SEQ],
                            ACT.Copy, scale=params[:, bass.ds(TILES * g + (PC_SSM_G + m), 1)]).then_inc(yz_hi, 1)
                return f

            def own_steps(g):
                n = N_G + g * (2 * NP_D)
                return {5: [seg_exponential(g, 0)], 8: [seg_exponential(g, 1)], 11: [seg_exponential(g, 2)],
                        14: [seg_exponential(g, 3)],
                        9: [copy_block(g + 4, n + NP_D, 0)],
                        10: [conv_first_tap(g + 4, g * TILES)],
                        13: [conv_silu(g + 4, x_conv)]}

            def last_steps(g):
                n = N_G + g * (2 * NP_D)
                return {1: [now(g)], 2: [keep_z(g, n + 2 * NP_D)], 5: [keep_state(g)], 9: [group_squares(g)],
                        10: [group_root(g)], 14: [keep_yz_hi(g)]}

            def both(a, b):
                return {k: a.get(k, []) + b.get(k, []) for k in sorted(set(a) | set(b))}

            stream(N_G, 2 * NP_D, both(c_steps(1), own_steps(0)))
            with act.Fori(0, GROUPS - 1) as g:
                stream((N_G + 2 * NP_D) + g * (2 * NP_D), 2 * NP_D, both(last_steps(g), own_steps(g + 1)))

            GATE_BANK, SECOND_BANK = 0, 2
            A_C, A_H, A_B = 0, 4, 6

            def gate(func, used, n_gate, freed, n_freed):
                def f():
                    act.wait_ge(weights_used, used)
                    if n_freed is not None:
                        act.wait_ge(freed, n_freed)
                    nc.scalar.activation(gate_val[:, :, :], blk2(GATE_BANK), func).then_inc(gate_done, 1)
                return f

            def keep_hi(dst, i, v):
                def f():
                    act.wait_ge(val_done, v + 1)
                    nc.scalar.activation(dst[:, bass.ds(TILES * i, TILES), 0, :], val[:, :, :], ACT.Copy)\
                        .then_inc(out_hi, 1)
                return f

            def os_own(i, first=False):
                n = N_OS + i * (NP_D + NP_I)
                return {10: [gate(ACT.Sigmoid, n + NP_D, i, mb_done, None if first else i)]}

            stream(N_OS, NP_D + NP_I, both(last_steps(GROUPS - 1), os_own(0, True)))
            with act.Fori(0, BLK_D - 1) as i:
                stream((N_OS + NP_D + NP_I) + i * (NP_D + NP_I), NP_D + NP_I, os_own(i + 1))

            def keep_c_part(i, first):
                def f():
                    act.wait_ge(weights_used, N_A + i * (3 * NP_D) + NP_D)
                    if not first:
                        act.wait_ge(ch_done, i)
                    nc.scalar.activation(a_c[:, :, :], blk2(A_C), ACT.Copy).then_inc(ac_kept, 1)
                return f

            def a_first_tap(i, first):
                def f():
                    act.wait_ge(ch_done, i + 1)
                    if not first:
                        act.wait_ge(val_done, i)
                    for m in range(TILES):
                        nc.scalar.activation(
                            a_conv[:, m, :], a_pre[:, m, CONV_A_K - 1:CONV_A_K - 1 + SEQ], ACT.Copy,
                            scale=params[:, bass.ds(TILES * i + (PC_CONV_A + (CONV_A_K - 1) * KD + m), 1)])\
                            .then_inc(a_first, 1)
                return f

            def a_own(i, first=False):
                return {10: [keep_c_part(i, first)], 19: [a_first_tap(i, first)]}

            stream(N_A, 3 * NP_D, a_own(0, True))
            with act.Fori(0, BLK_D - 1) as i:
                stream((N_A + 3 * NP_D) + i * (3 * NP_D), 3 * NP_D, both({3: [keep_hi(ya, i, i)]}, a_own(i + 1)))

            def oa_own(i, first=False):
                n = N_OA + i * (2 * NP_D)
                freed = (mb_done, BLK_D) if first else (val_done, BLK_D + i)
                return {10: [gate(ACT.Sigmoid, n + NP_D, BLK_D + i, *freed)]}

            stream(N_OA, 2 * NP_D, both({3: [keep_hi(ya, BLK_D - 1, BLK_D - 1)]}, oa_own(0, True)))
            with act.Fori(0, BLK_D - 1) as i:
                stream((N_OA + 2 * NP_D) + i * (2 * NP_D), 2 * NP_D,
                       both({3: [keep_hi(merged, i, i + BLK_D)]}, oa_own(i + 1)))

            stream(N_O, BLK_D * NP_D, {3: [keep_hi(merged, BLK_D - 1, 2 * BLK_D - 1)]})
            norm_stats(h_tok, 1)
            norm_hi(1, PC_FFN_G)

            def f_own(i):
                n = N_F + i * (2 * NP_D)
                return {10: [gate(ACT.Silu, n + NP_D, 2 * BLK_D + i, val_done, i + 2 * BLK_D)]}

            stream(N_F, 2 * NP_D, f_own(0))
            with act.Fori(0, BLK_F - 1) as i:
                stream((N_F + 2 * NP_D) + i * (2 * NP_D), 2 * NP_D,
                       both({3: [keep_hi(ff, i, i + 2 * BLK_D)]}, f_own(i + 1)))

            stream(N_DN, 2 * NP_F, {3: [keep_hi(ff, BLK_F - 1, 2 * BLK_D + BLK_F - 1)]})
            stream(N_DN + 2 * NP_F, 2 * NP_F, {})
            norm_stats(h_tok, 2)

        @block.vector
        def _(dve):
            def lo(n, c):
                s = c % SLOTS
                dve.wait_ge(weights_hi, n + 1)
                nc.vector.tensor_tensor(w_lo[s][:, :, :], raw[s][:, :, :], w_hi[s][:, :, :].bitcast(FP32),
                                        ALU.subtract).then_inc(weights_split, 1)

            def stream(n0, pieces, steps):
                for c in range(pieces):
                    lo(n0 + c, c)
                    for f in steps.get(c, []):
                        f()

            def both(a, b):
                return {k: a.get(k, []) + b.get(k, []) for k in sorted(set(a) | set(b))}

            def norm_rstd(k):
                dve.wait_ge(nrm_sum, CHUNKS * (k + 1))
                nc.vector.tensor_scalar(row_ms[:, :], row_sum[:, :], 1.0 / D_MODEL, EPS, ALU.mult, ALU.add)\
                    .then_inc(nrm_ms, 1)
                dve.wait_ge(nrm_rms, k + 1)
                nc.vector.reciprocal(row_rstd[:, :], row_rms[:, :]).then_inc(nrm_rstd, 1)
                dve.wait_ge(nrm_rstd, k + 1)

            def norm_scale(k, src, dst):
                norm_rstd(k)
                for c in range(CHUNKS):
                    nc.vector.tensor_scalar(dst[:, c, :], src[:, c, :], row_rstd[:, c:c + 1], None, ALU.mult)\
                        .then_inc(nrm_scaled, 1)

            def norm_lo(k, gcol):
                for b in range(KD // 2):
                    dve.wait_ge(nrm_hi, k * KD + 2 * b + 2)
                    for j in range(2):
                        t = 2 * b + j
                        nc.vector.scalar_tensor_tensor(
                            out=normed[:, t, 1, :], in0=ps[:, b, j * SEQ:(j + 1) * SEQ],
                            scalar=params[:, gcol + t:gcol + t + 1], in1=normed[:, t, 0, :].bitcast(FP32),
                            op0=ALU.mult, op1=ALU.subtract).then_inc(nrm_lo, 1)

            dve.wait_ge(masks_ready, 3)
            nc.vector.tensor_copy(after[:, :], after_f[:, :]).then_inc(after_ready, 1)
            dve.wait_ge(params_t, 1)
            nc.vector.tensor_copy(params[:, :], ps[:, 7, 0:PC_ALL]).then_inc(params_ready, 1)
            norm_scale(0, x_tok, x_nrm)
            dve.wait_ge(params_ready, 1)
            norm_lo(0, PC_MIX_G)
            dve.wait_ge(dtw_hi_ok, 1)
            nc.vector.tensor_tensor(dtw_lo[:, :, :], dtw_raw[:, :, :], dtw_hi[:, :, :].bitcast(FP32), ALU.subtract)\
                .then_inc(dtw_ready, 1)

            def dt_link(ins):
                ins.then_inc(dt_step, 1)
                dt_link.count += 1
                dve.wait_ge(dt_step, dt_link.count)
            dt_link.count = 0
            v, neg, nabs, a, den, rec, z, z2, p, pos = dt_tmp

            def by_chunk(ap):
                return ap.rearrange("p (c h) -> p c h", c=CHUNKS)

            def over_chunks(ap):
                return ap.unsqueeze(1).to_broadcast([P, CHUNKS, HEADS])

            def dt_argument():
                dve.wait_ge(dt_raw, 1)
                dve.wait_ge(heads_landed, 48)
                dt_link(nc.vector.tensor_tensor(by_chunk(v[:, :]), by_chunk(ps[:, 7, 0:CHUNKS * HEADS]),
                                                over_chunks(bias_b[:, :]), ALU.add))
                dt_link(nc.vector.tensor_scalar(neg[:, :], v[:, :], -1.0, None, ALU.mult))
                dt_link(nc.vector.tensor_tensor(nabs[:, :], v[:, :], neg[:, :], ALU.min))

            def dt_rest():
                dve.wait_ge(dt_exp, 1)
                dt_link(nc.vector.tensor_scalar(den[:, :], a[:, :], 2.0, None, ALU.add))
                dt_link(nc.vector.reciprocal(rec[:, :], den[:, :]))
                dt_link(nc.vector.tensor_tensor(z[:, :], a[:, :], rec[:, :], ALU.mult))
                dt_link(nc.vector.tensor_tensor(z2[:, :], z[:, :], z[:, :], ALU.mult))
                dt_link(nc.vector.tensor_scalar(p[:, :], z2[:, :], 1.0 / 19, None, ALU.mult))
                for odd in range(17, 1, -2):
                    dt_link(nc.vector.scalar_tensor_tensor(out=p[:, :], in0=p[:, :], scalar=1.0 / odd,
                                                           in1=z2[:, :], op0=ALU.add, op1=ALU.mult))
                dt_link(nc.vector.scalar_tensor_tensor(out=p[:, :], in0=p[:, :], scalar=1.0, in1=z[:, :],
                                                       op0=ALU.add, op1=ALU.mult))
                dt_link(nc.vector.tensor_scalar(pos[:, :], v[:, :], 0.0, None, ALU.max))
                dt_link(nc.vector.scalar_tensor_tensor(
                    out=dt[:, :, :].rearrange("p c h -> p (c h)"), in0=p[:, :], scalar=2.0, in1=pos[:, :],
                    op0=ALU.mult, op1=ALU.add))
                dve.wait_ge(heads_exp, 1)
                dt_link(nc.vector.scalar_tensor_tensor(out=loga[:, :, :], in0=dt[:, :, :], scalar=-1.0,
                                                       in1=over_chunks(anow_b[:, :]), op0=ALU.mult, op1=ALU.mult))
                dt_link(nc.vector.tensor_copy(loga_hi[:, :, :], loga[:, :, :]))
                dt_link(nc.vector.tensor_tensor(loga_lo[:, :, :], loga[:, :, :],
                                                loga_hi[:, :, :].bitcast(FP32), ALU.subtract))

            def conv_tap(q, tile, j):
                def f():
                    before = 12 * q + 4 * (CONV_K - 2 - j)
                    for m in range(TILES):
                        if j == CONV_K - 2:
                            dve.wait_ge(conv_first, 4 * q + m + 1)
                        else:
                            dve.wait_ge(conv_taps, before - 4 + m + 1)
                        nc.vector.scalar_tensor_tensor(
                            out=x_conv[:, m, :], in0=x_pre[:, m, j:j + SEQ],
                            scalar=params[:, bass.ds(tile + (PC_CONV_W + j * CONV_TILES + m), 1)],
                            in1=x_conv[:, m, :], op0=ALU.mult, op1=ALU.add).then_inc(conv_taps, 1)
                return f

            def keep_cb(i):
                def f():
                    dve.wait_ge(cb_ready, i + 1)
                    for c in range(CHUNKS):
                        nc.vector.tensor_tensor(cb[:, TILES * i:TILES * (i + 1), c, :],
                                                ps[:, 6 + c, :].rearrange("p (g l) -> p g l", l=P),
                                                upto[:, :].unsqueeze(1).to_broadcast([P, TILES, P]), ALU.mult)\
                            .then_inc(cb_kept, 1)
                return f

            B_TILE, C_TILE = D_INNER // P, D_INNER // P + GROUPS

            def conv_steps(q, tile, s):
                return {s: [conv_tap(q, tile, 2)], s + 1: [conv_tap(q, tile, 1)], s + 2: [conv_tap(q, tile, 0)]}

            def c_steps(i):
                return both(conv_steps(2 * i + 1, C_TILE + TILES * i, 2), {9: [keep_cb(i)]})

            for i in range(2):
                steps = conv_steps(2 * i, B_TILE + TILES * i, 10)
                steps = both(steps, {0: [dt_argument], 4: [dt_rest]} if i == 0 else c_steps(0))
                stream(N_BC + 2 * i * NP_D, 2 * NP_D, steps)

            def seg_input(g, b):
                c, h = b // 2, HEADS_G * g + 4 * (b % 2)
                def f():
                    if not (isinstance(g, int) and g == 0 and b == 0):
                        dve.wait_ge(seg_ready, 4 * g + b)
                    else:
                        dve.wait_ge(dt_step, dt_link.count)
                    for dst, src in ((seg_hi, loga_hi), (seg_lo, loga_lo)):
                        nc.vector.tensor_tensor(
                            dst[:, :, :], upto[:, :].unsqueeze(1).to_broadcast([P, 4, P]),
                            src[:, c, bass.ds(h, 4)].bitcast(FP32).unsqueeze(2).to_broadcast([P, 4, P]), ALU.mult)\
                            .then_inc(seg_in, 1)
                return f

            def seg_mix(g, b):
                def f():
                    dve.wait_ge(seg_exp, 4 * g + b + 1)
                    nc.vector.tensor_tensor(
                        mix[:, b, :, :], mix[:, b, :, :],
                        cb[:, bass.ds(g, 1), b // 2, :].to_broadcast([P, 4, P]), ALU.mult).then_inc(mix_ready, 1)
                return f

            def prepare_x(g):
                def f():
                    dve.wait_ge(x_t, 2 * g + 2)
                    dve.wait_ge(decays_ready, 2)
                    if not (isinstance(g, int) and g == 0):
                        dve.wait_ge(yz_t, 2 * g)
                    for c in range(CHUNKS):
                        nc.vector.tensor_tensor(heads_of(y[:, c, :]), heads_of(ps[:, 6 + c, :]),
                                                per_head(skip_b[:, bass.ds(HEADS_G * g, HEADS_G)]), ALU.mult)\
                            .then_inc(xprep, 1)
                        nc.vector.tensor_tensor(heads_of(xdt[:, c, :]), heads_of(ps[:, 6 + c, :]),
                                                per_head(dt[:, c, bass.ds(HEADS_G * g, HEADS_G)]), ALU.mult)\
                            .then_inc(xprep, 1)
                    dve.wait_ge(xprep, 5 * g + 4)
                    nc.vector.tensor_tensor(heads_of(xdec[:, :]), heads_of(xdt[:, 0, :]),
                                            per_head(dec_end[:, bass.ds(HEADS_G * g, HEADS_G)]), ALU.mult)\
                        .then_inc(xprep, 1)
                return f

            def sum_first(g):
                def f():
                    dve.wait_ge(y_first, g + 1)
                    nc.vector.tensor_tensor(y[:, 0, :], y[:, 0, :], ps[:, 7, :], ALU.add).then_inc(y_sum, 1)
                return f

            def sum_second(g):
                def f():
                    dve.wait_ge(y_second, g + 1)
                    nc.vector.tensor_tensor(heads_of(xdec[:, :]), heads_of(ps[:, 6, :]),
                                            per_head(dec_in[:, bass.ds(HEADS_G * g, HEADS_G)]), ALU.mult)\
                        .then_inc(y_sum, 1)
                    nc.vector.tensor_tensor(y[:, 1, :], y[:, 1, :], ps[:, 7, :], ALU.add).then_inc(y_sum, 1)
                    dve.wait_ge(z_kept, g + 1)
                    dve.wait_ge(y_sum, 6 * g + 1)
                    nc.vector.tensor_tensor(y[:, 0, :], y[:, 0, :], z_act[:, 0, :], ALU.mult).then_inc(y_sum, 1)
                    dve.wait_ge(y_sum, 6 * g + 3)
                    nc.vector.tensor_tensor(y[:, 1, :], y[:, 1, :], xdec[:, :], ALU.add).then_inc(y_sum, 1)
                    dve.wait_ge(y_sum, 6 * g + 5)
                    nc.vector.tensor_tensor(y[:, 1, :], y[:, 1, :], z_act[:, 1, :], ALU.mult).then_inc(y_sum, 1)
                return f

            def group_mean(g):
                def f():
                    dve.wait_ge(g_sq, 2 * g + 2)
                    nc.vector.tensor_scalar(grp_ms[:, :], grp_sum[:, :], 1.0 / COLS, EPS, ALU.mult, ALU.add)\
                        .then_inc(g_ms, 1)
                return f

            def group_scale(g):
                def f():
                    dve.wait_ge(g_rms, g + 1)
                    nc.vector.reciprocal(grp_rstd[:, :], grp_rms[:, :]).then_inc(g_rstd, 1)
                    dve.wait_ge(g_rstd, g + 1)
                    for c in range(CHUNKS):
                        nc.vector.tensor_scalar(y[:, c, :], y[:, c, :], grp_rstd[:, c:c + 1], None, ALU.mult)\
                            .then_inc(g_scaled, 1)
                return f

            def keep_yz_lo(g):
                def f():
                    for m in range(TILES):
                        dve.wait_ge(yz_hi, 4 * g + 2 * (m // 2) + 2)
                        nc.vector.scalar_tensor_tensor(
                            out=yz[:, bass.ds(TILES * g + m, 1), 1, :].rearrange("p a t -> p (a t)"),
                            in0=ps[:, 6 + m // 2, (m % 2) * SEQ:(m % 2 + 1) * SEQ],
                            scalar=params[:, bass.ds(TILES * g + (PC_SSM_G + m), 1)],
                            in1=yz[:, bass.ds(TILES * g + m, 1), 0, :].rearrange("p a t -> p (a t)").bitcast(FP32),
                            op0=ALU.mult, op1=ALU.subtract).then_inc(yz_lo, 1)
                return f

            def own_steps(g):
                seg = {2 + 3 * b: [seg_input(g, b)] for b in range(4)}
                mixes = {5 + 3 * b: [seg_mix(g, b)] for b in range(4)}
                return both(both(mixes, seg), conv_steps(g + 4, g * TILES, 10))

            def last_steps(g):
                return {1: [prepare_x(g)], 5: [sum_first(g)], 8: [sum_second(g)], 9: [group_mean(g)],
                        10: [group_scale(g)], 14: [keep_yz_lo(g)]}

            stream(N_G, 2 * NP_D, both(c_steps(1), own_steps(0)))
            with dve.Fori(0, GROUPS - 1) as g:
                stream((N_G + 2 * NP_D) + g * (2 * NP_D), 2 * NP_D, both(last_steps(g), own_steps(g + 1)))

            SECOND_BANK, A_H, A_B = 2, 4, 6

            def value(bank, other, used, v, first, done, n_done, sem_out):
                def f():
                    dve.wait_ge(weights_used, used)
                    dve.wait_ge(done, n_done)
                    if not first:
                        dve.wait_ge(out_hi, v)
                        dve.wait_ge(out_lo, v)
                    nc.vector.tensor_tensor(val[:, :, :], blk2(bank), other[:, :, :], ALU.mult).then_inc(sem_out, 1)
                return f

            def keep_lo(dst, i, v):
                def f():
                    dve.wait_ge(out_hi, v + 1)
                    nc.vector.tensor_tensor(dst[:, bass.ds(TILES * i, TILES), 1, :], val[:, :, :],
                                            dst[:, bass.ds(TILES * i, TILES), 0, :].bitcast(FP32), ALU.subtract)\
                        .then_inc(out_lo, 1)
                return f

            def keep_merged_b(i):
                def f():
                    dve.wait_ge(weights_used, N_OS + (NP_D + NP_I) + i * (NP_D + NP_I))
                    dve.wait_ge(gate_done, i + 1)
                    nc.vector.tensor_tensor(merged_b[:, bass.ds(TILES * i, TILES), :], blk2(SECOND_BANK),
                                            gate_val[:, :, :], ALU.mult).then_inc(mb_done, 1)
                return f

            stream(N_OS, NP_D + NP_I, last_steps(GROUPS - 1))
            with dve.Fori(0, BLK_D - 1) as i:
                stream((N_OS + NP_D + NP_I) + i * (NP_D + NP_I), NP_D + NP_I, {2: [keep_merged_b(i)]})

            def product_ch(i, first):
                def f():
                    dve.wait_ge(weights_used, N_A + 2 * NP_D + i * (3 * NP_D))
                    dve.wait_ge(ac_kept, i + 1)
                    if first:
                        dve.wait_ge(pads_zero, 2)
                    else:
                        dve.wait_ge(a_taps, 8 * i)
                    nc.vector.tensor_tensor(a_pre[:, :, CONV_A_K - 1:CONV_A_K - 1 + SEQ], blk2(A_H),
                                            a_c[:, :, :], ALU.mult).then_inc(ch_done, 1)
                return f

            def a_tap(i, j):
                def f():
                    for m in range(TILES):
                        if j == CONV_A_K - 2:
                            dve.wait_ge(a_first, 4 * i + m + 1)
                        else:
                            dve.wait_ge(a_taps, 8 * i + m + 1)
                        nc.vector.scalar_tensor_tensor(
                            out=a_conv[:, m, :], in0=a_pre[:, m, j:j + SEQ],
                            scalar=params[:, bass.ds(TILES * i + (PC_CONV_A + j * KD + m), 1)],
                            in1=a_conv[:, m, :], op0=ALU.mult, op1=ALU.add).then_inc(a_taps, 1)
                return f

            def a_own(i, first=False):
                return {18: [product_ch(i, first)], 20: [a_tap(i, 1)], 21: [a_tap(i, 0)]}

            def a_last(i, first=False):
                return {2: [value(A_B, a_conv, N_A + 3 * NP_D + i * (3 * NP_D), i, first, a_taps, 8 * i + 8, val_done)],
                        3: [keep_lo(ya, i, i)]}

            stream(N_A, 3 * NP_D, both({2: [keep_merged_b(BLK_D - 1)]}, a_own(0, True)))
            stream(N_A + 3 * NP_D, 3 * NP_D, both(a_last(0, True), a_own(1)))
            with dve.Fori(0, BLK_D - 2) as i:
                stream((N_A + 6 * NP_D) + i * (3 * NP_D), 3 * NP_D, both(a_last(i + 1), a_own(i + 2)))

            def add_merged_b(i):
                def f():
                    dve.wait_ge(val_part, i + 1)
                    nc.vector.tensor_tensor(val[:, :, :], val[:, :, :], merged_b[:, bass.ds(TILES * i, TILES), :],
                                            ALU.add).then_inc(val_done, 1)
                return f

            def oa_last(i):
                return {2: [value(SECOND_BANK, gate_val, N_OA + 2 * NP_D + i * (2 * NP_D), i + BLK_D, False,
                                  gate_done, i + BLK_D + 1, val_part), add_merged_b(i)],
                        3: [keep_lo(merged, i, i + BLK_D)]}

            stream(N_OA, 2 * NP_D, a_last(BLK_D - 1))
            with dve.Fori(0, BLK_D - 1) as i:
                stream((N_OA + 2 * NP_D) + i * (2 * NP_D), 2 * NP_D, oa_last(i))

            stream(N_O, BLK_D * NP_D, oa_last(BLK_D - 1))
            dve.wait_ge(x2_landed, 16 * CHUNKS)
            for c in range(BLK_D):
                dve.wait_ge(weights_used, N_F - (BLK_D - 1) + c)
                for t in range(CHUNKS):
                    nc.vector.tensor_tensor(h_tok[:, t, c * COLS:(c + 1) * COLS], ps[:, (4 + 2 * c) % 8 + t, :],
                                            x_res[:, t, c * COLS:(c + 1) * COLS], ALU.add).then_inc(o_summed, 1)
            norm_scale(1, h_tok, h_nrm)
            norm_lo(1, PC_FFN_G)

            def f_last(i):
                v = i + 2 * BLK_D
                return {2: [value(SECOND_BANK, gate_val, N_F + 2 * NP_D + i * (2 * NP_D), v, False,
                                  gate_done, v + 1, val_done)],
                        3: [keep_lo(ff, i, v)]}

            stream(N_F, 2 * NP_D, {})
            with dve.Fori(0, BLK_F - 1) as i:
                stream((N_F + 2 * NP_D) + i * (2 * NP_D), 2 * NP_D, f_last(i))

            def sum_down(c):
                def f():
                    dve.wait_ge(weights_used, N_DN + (c + 1) * NP_F)
                    for t in range(CHUNKS):
                        nc.vector.tensor_tensor(h_tok[:, t, c * COLS:(c + 1) * COLS],
                                                h_tok[:, t, c * COLS:(c + 1) * COLS], ps[:, (4 + 2 * c) % 8 + t, :],
                                                ALU.add).then_inc(d_summed, 1)
                return f

            stream(N_DN, 2 * NP_F, both(f_last(BLK_F - 1), {NP_F + 2: [sum_down(0)]}))
            stream(N_DN + 2 * NP_F, 2 * NP_F, {2: [sum_down(1)], NP_F + 2: [sum_down(2)]})
            sum_down(3)()
            norm_rstd(2)
            dve.wait_ge(final_landed, 16)
            for c in range(CHUNKS):
                nc.vector.scalar_tensor_tensor(out=y_out[:, c, :], in0=h_tok[:, c, :], scalar=row_rstd[:, c:c + 1],
                                               in1=final_b[:, :], op0=ALU.mult, op1=ALU.mult).then_inc(fin_ready, 1)

        @block.tensor
        def _(pe):
            def features(src, k0, bank, c, k_all):
                def f():
                    s = c % SLOTS
                    for m in range(TILES):
                        out_m = ps[:, bank + m // 2, (m % 2) * SEQ:(m % 2 + 1) * SEQ]
                        for kk in range(KP):
                            k = c * KP + kk - k0
                            hi_w = w_hi[s][:, kk, m * P:(m + 1) * P]
                            lo_w = w_lo[s][:, kk, m * P:(m + 1) * P]
                            nc.tensor.matmul(out_m, hi_w, src[:, k, 0, :], start=(k == 0 and m % 2 == 0), stop=False,
                                             skip_group_check=True)
                            nc.tensor.matmul(out_m, hi_w, src[:, k, 1, :], start=False, stop=False,
                                             skip_group_check=True)
                            last = nc.tensor.matmul(out_m, lo_w, src[:, k, 0, :], start=False, stop=(k == k_all - 1),
                                                    skip_group_check=True)
                    return last
                return f

            def tokens(src, k0, bank, c, k_all):
                def f():
                    s = c % SLOTS
                    for t in range(CHUNKS):
                        out_t = ps[:, bank + t, :]
                        for kk in range(KP):
                            k = k0 + kk
                            hi_a = src[:, k, 0, t * P:(t + 1) * P]
                            lo_a = src[:, k, 1, t * P:(t + 1) * P]
                            nc.tensor.matmul(out_t, hi_a, w_hi[s][:, kk, :], start=(k == 0), stop=False)
                            nc.tensor.matmul(out_t, hi_a, w_lo[s][:, kk, :], start=False, stop=False)
                            last = nc.tensor.matmul(out_t, lo_a, w_hi[s][:, kk, :], start=False, stop=(k == k_all - 1))
                    return last
                return f

            def stream(n0, products, steps):
                for c, multiply in enumerate(products):
                    for f in steps.get(c, []):
                        f()
                    pe.wait_ge(weights_split, n0 + c + 1)
                    multiply().then_inc(weights_used, 1)

            def both(a, b):
                return {k: a.get(k, []) + b.get(k, []) for k in sorted(set(a) | set(b))}

            def feature_block(src, bank, pieces, c0=0):
                return [features(src, c0 * KP, bank, c0 + c, pieces * KP) for c in range(pieces)]

            def token_block(src, bank, pieces, c0=0):
                return [(lambda c=c: tokens(src, c * KP, bank, c0 + c, pieces * KP)()) for c in range(pieces)]

            def wait(s, v):
                return lambda: pe.wait_ge(s, v)

            def norm_transpose(k, src):
                for b in range(KD // 2):
                    if k == 0 and b == 7:
                        pe.wait_ge(params_ready, 1)
                    for j in range(2):
                        for c in range(CHUNKS):
                            if b == 0 and j == 0:
                                pe.wait_ge(nrm_scaled, CHUNKS * (k + 1))
                            t = 2 * b + j
                            last = nc.tensor.transpose(ps[:, b, j * SEQ + c * P:j * SEQ + (c + 1) * P],
                                                       src[:, c, t * P:(t + 1) * P], ident[:, :])
                    last.then_inc(nrm_t, 1)

            pe.wait_ge(masks_ready, 3)
            pe.wait_ge(rows_landed, 16 * len(parameter_loads))
            for j in range(PC_TABLES):
                n = min(P, PC_ALL - j * P)
                last = nc.tensor.transpose(ps[:, 7, j * P:j * P + n], par_rows[0:n, j, :], ident[0:n, 0:n])
            last.then_inc(params_t, 1)
            norm_transpose(0, x_nrm)
            pe.wait_ge(nrm_lo, KD)
            pe.wait_ge(dtw_ready, 1)
            for c in range(CHUNKS):
                for k in range(KD):
                    o = ps[:, 7, c * HEADS:(c + 1) * HEADS]
                    hi_a, lo_a = normed[:, k, 0, c * P:(c + 1) * P], normed[:, k, 1, c * P:(c + 1) * P]
                    nc.tensor.matmul(o, hi_a, dtw_hi[:, k, :], start=(k == 0), stop=False)
                    nc.tensor.matmul(o, hi_a, dtw_lo[:, k, :], start=False, stop=False)
                    last = nc.tensor.matmul(o, lo_a, dtw_hi[:, k, :], start=False, stop=(k == KD - 1))
            last.then_inc(dt_raw, 1)

            def running_sums():
                pe.wait_ge(dt_step, 20)
                nc.tensor.matmul(ps[:, 7, 0:HEADS], after_f[:, :], loga[:, 0, :], start=True, stop=True)
                nc.tensor.matmul(ps[:, 7, HEADS:2 * HEADS], upto[:, :], loga[:, 1, :], start=True, stop=True)\
                    .then_inc(cs_ready, 1)

            def transpose_b(i):
                def f():
                    pe.wait_ge(conv_act, 2 * i + 1)
                    if i:
                        pe.wait_ge(cb_kept, 2)
                    for m in range(TILES):
                        last = nc.tensor.transpose(ps[:, 6, m * P:(m + 1) * P], b_feat[:, m, 0:P], ident[:, :])
                    last.then_inc(b_t, 1)
                return f

            def multiply_cb(i):
                def f():
                    pe.wait_ge(conv_act, 2 * i + 2)
                    pe.wait_ge(b_kept, i + 1)
                    pe.wait_ge(decays_ready, 2)
                    for c in range(CHUNKS):
                        for m in range(TILES):
                            last = nc.tensor.matmul(ps[:, 6 + c, m * P:(m + 1) * P], b_feat[:, m, c * P:(c + 1) * P],
                                                    c_feat[:, m, c * P:(c + 1) * P], start=True, stop=True)
                    last.then_inc(cb_ready, 1)
                return f

            for i in range(2):
                steps = {15: [transpose_b(i)]}
                if i == 0:
                    steps |= {5: [running_sums]}
                else:
                    steps |= {0: [wait(acc_copied, 1)], 7: [multiply_cb(0)], 8: [wait(acc_copied, 2)]}
                stream(N_BC + 2 * i * NP_D,
                       feature_block(normed, 0, NP_D) + feature_block(normed, 4, NP_D, NP_D), steps)

            def segment(g, b):
                def f():
                    pe.wait_ge(seg_in, 8 * g + 2 * b + 2)
                    if not (isinstance(g, int) and g == 0 and b < 2):
                        pe.wait_ge(seg_exp, 4 * g + b - 1)
                    else:
                        pe.wait_ge(after_ready, 1)
                    nc.tensor.matmul(ps[:, 2 + b % 2, :], after[:, :], seg_hi[:, :, :].rearrange("p h l -> p (h l)"),
                                     start=True, stop=False)
                    nc.tensor.matmul(ps[:, 2 + b % 2, :], after[:, :], seg_lo[:, :, :].rearrange("p h l -> p (h l)"),
                                     start=False, stop=True).then_inc(seg_ready, 1)
                return f

            def transpose_x(g):
                def f():
                    pe.wait_ge(conv_act, g + 5)
                    if isinstance(g, int) and g == 0:
                        pe.wait_ge(cb_kept, 4)
                    else:
                        pe.wait_ge(yz_lo, 4 * g)
                    for c in range(CHUNKS):
                        for m in range(TILES):
                            last = nc.tensor.transpose(ps[:, 6 + c, m * P:(m + 1) * P],
                                                       x_conv[:, m, c * P:(c + 1) * P], ident[:, :])
                        last.then_inc(x_t, 1)
                return f

            def own_products(c):
                for h in range(HEADS_G):
                    last = nc.tensor.matmul(ps[:, 7, h * HEAD_DIM:(h + 1) * HEAD_DIM], mix[:, 2 * c + h // 4, h % 4, :],
                                            xdt[:, c, h * HEAD_DIM:(h + 1) * HEAD_DIM], start=True, stop=True)
                return last

            def first_chunk(g):
                def f():
                    pe.wait_ge(xprep, 5 * g + 5)
                    pe.wait_ge(now_kept, 2 * g + 2)
                    pe.wait_ge(mix_ready, 4 * g + 2)
                    nc.tensor.matmul(ps[:, 6, :], b_now[:, :], xdec[:, :], start=True, stop=True)
                    own_products(0).then_inc(y_first, 1)
                return f

            def second_chunk(g):
                def f():
                    pe.wait_ge(state_kept, g + 1)
                    pe.wait_ge(y_sum, 6 * g + 1)
                    pe.wait_ge(mix_ready, 4 * g + 4)
                    nc.tensor.matmul(ps[:, 6, :], c_now[:, :], state_sb[:, :], start=True, stop=True)
                    own_products(1).then_inc(y_second, 1)
                return f

            def transpose_yz(g):
                def f():
                    pe.wait_ge(g_scaled, 2 * g + 2)
                    for b in range(2):
                        for j in range(2):
                            for c in range(CHUNKS):
                                m = 2 * b + j
                                last = nc.tensor.transpose(ps[:, 6 + b, j * SEQ + c * P:j * SEQ + (c + 1) * P],
                                                           y[:, c, m * P:(m + 1) * P], ident[:, :])
                        last.then_inc(yz_t, 1)
                return f

            def own_steps(g):
                steps = {3 + 3 * b: [segment(g, b)] for b in range(4)}
                return both(steps, {0: [wait(acc_copied, g + 4)], 15: [transpose_x(g)]})

            def last_steps(g):
                return {3: [first_chunk(g)], 6: [second_chunk(g)], 12: [transpose_yz(g)]}

            group_products = feature_block(normed, 0, NP_D) + token_block(normed, 4, NP_D, NP_D)
            stream(N_G, group_products, both(own_steps(0), {7: [multiply_cb(1)], 8: [wait(acc_copied, 4)]}))
            with pe.Fori(0, GROUPS - 1) as g:
                stream((N_G + 2 * NP_D) + g * (2 * NP_D), group_products,
                       both(both(last_steps(g), own_steps(g + 1)), {8: [wait(z_kept, g + 1)]}))

            os_products = feature_block(normed, 0, NP_D) + feature_block(yz, 2, NP_I, NP_D)
            stream(N_OS, os_products,
                   both(last_steps(GROUPS - 1),
                        {0: [wait(acc_copied, 4 + GROUPS)],
                         8: [wait(seg_exp, 4 * GROUPS)],
                         8 + NP_I - KP: [wait(yz_lo, 4 * GROUPS)]}))
            with pe.Fori(0, BLK_D - 1) as i:
                stream((N_OS + NP_D + NP_I) + i * (NP_D + NP_I), os_products,
                       {0: [wait(gate_done, i + 1)], 8: [wait(mb_done, i + 1)]})

            a_products = (feature_block(normed, 0, NP_D) + feature_block(normed, 4, NP_D, NP_D)
                          + feature_block(normed, 6, NP_D, 2 * NP_D))
            stream(N_A, a_products, {0: [wait(gate_done, BLK_D)], 8: [wait(z_kept, GROUPS)]})
            with pe.Fori(0, BLK_D - 1) as i:
                stream((N_A + 3 * NP_D) + i * (3 * NP_D), a_products,
                       {0: [wait(ac_kept, i + 1)], 8: [wait(ch_done, i + 1)], 16: [wait(val_done, i + 1)]})

            oa_products = feature_block(normed, 0, NP_D) + feature_block(ya, 2, NP_D, NP_D)
            stream(N_OA, oa_products, {0: [wait(ac_kept, BLK_D)], 8: [wait(mb_done, BLK_D), wait(out_lo, BLK_D)]})
            with pe.Fori(0, BLK_D - 1) as i:
                stream((N_OA + 2 * NP_D) + i * (2 * NP_D), oa_products,
                       {0: [wait(gate_done, i + BLK_D + 1)], 8: [wait(val_part, i + 1)]})

            o_products = [(lambda c=c, k=k: tokens(merged, k * KP, (4 + 2 * c) % 8, c, KD)())
                          for k in range(NP_D) for c in range(BLK_D)]
            stream(N_O, o_products,
                   {0: [wait(out_lo, 2 * BLK_D - 1), wait(val_done, BLK_D)], 2: [wait(gate_done, 2 * BLK_D)],
                    3: [wait(val_part, BLK_D)], BLK_D * (NP_D - 2): [wait(out_lo, 2 * BLK_D)]})
            pe.wait_ge(o_summed, 2 * BLK_D)
            norm_transpose(1, h_nrm)
            pe.wait_ge(nrm_lo, 2 * KD)

            f_products = feature_block(normed, 0, NP_D) + feature_block(normed, 2, NP_D, NP_D)
            stream(N_F, f_products, {})
            with pe.Fori(0, BLK_F - 1) as i:
                stream((N_F + 2 * NP_D) + i * (2 * NP_D), f_products,
                       {0: [wait(gate_done, i + 2 * BLK_D + 1)], 8: [wait(val_done, i + 2 * BLK_D + 1)]})

            for i in range(BLK_D // 2):
                products = (token_block(ff, (4 + 4 * i) % 8, NP_F) + token_block(ff, (6 + 4 * i) % 8, NP_F, NP_F))
                steps = {0: [wait(nrm_lo, 2 * KD)]} if i == 0 else {}
                if i == 0:
                    steps[NP_F - 2] = [wait(out_lo, 2 * BLK_D + BLK_F)]
                else:
                    steps[0] = [wait(val_done, 2 * BLK_D + BLK_F)]
                stream(N_DN + i * 2 * NP_F, products, steps)


_INS = ["x", "norm_mix_g", "w_in", "conv_a_w", "w_out_a", "ssm_conv_w", "ssm_conv_b", "dt_bias", "a_log", "d_skip",
        "ssm_norm_g", "w_out_ssm", "w_o", "norm_ffn_g", "w_ffn_gate", "w_ffn_up", "w_ffn_down", "norm_final_g"]
_OUTS = [((1, SEQ, D_MODEL), "float32")]


def kernel(**inputs):
    import numpy as _np
    import concourse.bacc as _bacc
    from concourse import mybir as _mybir
    from concourse.bass_utils import run_bass_kernel_spmd as _run

    nc = _bacc.Bacc("TRN2", target_bir_lowering=False, num_devices=1)
    arrays, args = {}, []
    for name in _INS:
        a = _np.ascontiguousarray(inputs[name])
        arrays[f"in_{name}_dram"] = a
        args.append(nc.dram_tensor(f"in_{name}_dram", a.shape, _mybir.dt.from_np(a.dtype), kind="ExternalInput").ap())
    for i, (shape, dtype) in enumerate(_OUTS):
        dt = _mybir.dt.from_np(_np.dtype(dtype))
        args.append(nc.dram_tensor(f"out_{i}_dram", shape, dt, kind="ExternalOutput").ap())
    hybrid_block_kernel(nc, *args)
    r = _run(nc, [arrays], core_ids=[0])
    return r.results[0]["out_0_dram"]
```

```python
import concourse.bass as bass
from concourse import mybir
from contextlib import ExitStack
import numpy as np

FP32 = mybir.dt.float32
FP32R = mybir.dt.float32r
ALU = mybir.AluOpType
ACT = mybir.ActivationFunctionType

P = 128
D_MODEL = 2048
SEQ = 256
EPS = 1e-6
D_INNER = 2 * D_MODEL
HEAD_DIM = 64
HEADS = D_INNER // HEAD_DIM
GROUPS = 8
HEADS_G = HEADS // GROUPS
STATE = 128
CONV_DIM = D_INNER + 2 * GROUPS * STATE
CONV_K = 4
CONV_A_K = 3
D_FF = -(-(8 * D_MODEL) // (3 * 256)) * 256
OFF_GATE_A = 0
OFF_GATE_B = D_MODEL
OFF_A = 2 * D_MODEL
OFF_Z = OFF_A + 3 * D_MODEL
OFF_XBC = OFF_Z + D_INNER
OFF_DT = OFF_XBC + CONV_DIM

COLS = 512
TILES = COLS // P
WARM_UP = 32
KP = 2
SLOTS = 4
CHUNKS = SEQ // P
KD = D_MODEL // P
KF = D_FF // P
NP_D = KD // KP
NP_I = 2 * KD // KP
NP_F = KF // KP
BLK_D = D_MODEL // COLS
BLK_F = D_FF // COLS
DVE_COLS = 5 * D_MODEL // 8

CONV_TILES = CONV_DIM // P
PC_CONV_W = 0
PC_CONV_B = PC_CONV_W + CONV_K * CONV_TILES
PC_MIX_G = PC_CONV_B + CONV_TILES
PC_CONV_A = PC_MIX_G + KD
PC_SSM_G = PC_CONV_A + CONV_A_K * KD
PC_FFN_G = PC_SSM_G + 2 * KD
PC_ALL = PC_FFN_G + KD
PC_TABLES = -(-PC_ALL // P)

N_BC = 0
N_G = N_BC + 4 * NP_D
N_OS = N_G + GROUPS * 2 * NP_D
N_A = N_OS + BLK_D * (NP_D + NP_I)
N_OA = N_A + BLK_D * 3 * NP_D
N_O = N_OA + BLK_D * 2 * NP_D
N_F = N_O + BLK_D * NP_D
N_DN = N_F + BLK_F * 2 * NP_D
N_END = N_DN + BLK_D * NP_F


def hybrid_block_kernel(nc, x, norm_mix_g, w_in, conv_a_w, w_out_a, ssm_conv_w, ssm_conv_b, dt_bias,
                        a_log, d_skip, ssm_norm_g, w_out_ssm, w_o, norm_ffn_g, w_ffn_gate, w_ffn_up,
                        w_ffn_down, norm_final_g, out):
    ctx = ExitStack()
    with ctx:
        KIB = 1024
        BASE = -(-nc.sbuf_base // 64) * 64
        assert BASE + 207 * KIB + 512 <= nc.sbuf_usable_end

        def at(name, kib, shape, dt=FP32):
            return nc.alloc_sbuf_tensor_at(name, shape, dt, offset=BASE + int(kib * KIB))

        raw = [at(f"weights_raw{s}", 4 * s, [P, KP, COLS]) for s in range(SLOTS)]
        w_hi = [at(f"weights_hi{s}", 16 + 4 * s, [P, KP, COLS], FP32R) for s in range(SLOTS)]
        w_lo = [at(f"weights_lo{s}", 32 + 4 * s, [P, KP, COLS], FP32R) for s in range(SLOTS)]
        normed = at("normed", 48, [P, KD, 2, SEQ], FP32R)
        Q, R, CO, W = 80, 168, 184, 189

        params = at("params", CO, [P, PC_ALL])
        ident = at("ident", CO + 1.5, [P, P])
        upto = at("upto", CO + 2, [P, P])
        after = at("after", CO + 2.5, [P, P], FP32R)
        after_f = at("after_f", CO + 3, [P, P])
        row_part = at("row_part", CO + 4.5, [P, CHUNKS, BLK_D])
        zero = at("zero", CO + 4.75, [P, 1])
        root = at("root", CO + 4.75 + 1 / 16, [P, 1])
        row_sum = at("row_sum", CO + 3.5, [P, CHUNKS])
        row_ms = at("row_ms", CO + 3.5 + 1 / 16, [P, CHUNKS])
        row_rms = at("row_rms", CO + 3.5 + 2 / 16, [P, CHUNKS])
        row_rstd = at("row_rstd", CO + 3.5 + 3 / 16, [P, CHUNKS])
        grp_sum = at("grp_sum", CO + 3.5 + 4 / 16, [P, CHUNKS])
        grp_ms = at("grp_ms", CO + 3.5 + 5 / 16, [P, CHUNKS])
        grp_rms = at("grp_rms", CO + 3.5 + 6 / 16, [P, CHUNKS])
        grp_rstd = at("grp_rstd", CO + 3.5 + 7 / 16, [P, CHUNKS])

        x_tok = at("x_tok", Q, [P, CHUNKS, D_MODEL])
        x_nrm = at("x_nrm", Q + 16, [P, CHUNKS, D_MODEL])
        par_rows = at("par_rows", Q + 32, [P, PC_TABLES, P])
        dtw_raw = at("dtw_raw", Q + 34, [P, KD, HEADS])
        dtw_hi = at("dtw_hi", Q + 38, [P, KD, HEADS], FP32R)
        dtw_lo = at("dtw_lo", Q + 60, [P, KD, HEADS], FP32R)
        dt_cols = at("dt_cols", Q + 44, [HEADS, SEQ])
        dt_half = at("dt_half", Q + 45, [HEADS, SEQ])
        dt_tmp = [at(f"dt_tmp{j}", Q + 46 + j / 2, [P, CHUNKS * HEADS]) for j in range(10)]
        bias_b = at("bias_b", Q + 52, [P, HEADS])
        alog_b = at("alog_b", Q + 52.25, [P, HEADS])
        anow_b = at("anow_b", Q + 52.5, [P, HEADS])
        loga = at("loga", Q + 53, [P, CHUNKS, HEADS])

        yz = at("yz", Q, [P, 2 * KD, 2, SEQ], FP32R)
        b_feat = at("b_feat", Q + 56, [P, TILES, SEQ])
        c_feat = at("c_feat", Q + 60, [P, TILES, SEQ])
        S = Q + 64
        cb = at("cb", S, [P, GROUPS, CHUNKS, P])
        c_last = at("c_last", S + 8, [P, GROUPS, P])
        b_first = at("b_first", S + 12, [P, GROUPS, STATE])
        x_pre = at("x_pre", S + 16, [P, TILES, SEQ + CONV_K])
        x_conv = at("x_conv", S + 20.25, [P, TILES, SEQ])
        xdt = at("xdt", S + 24.25, [P, CHUNKS, COLS])
        y = at("y", S + 28.25, [P, CHUNKS, COLS])
        xdec = at("xdec", S + 32.25, [P, COLS])
        state_sb = at("state_sb", S + 34.25, [P, COLS])
        dt = at("dt", S + 36.25, [P, CHUNKS, HEADS])
        loga_hi = at("loga_hi", S + 36.75, [P, CHUNKS, HEADS], FP32R)
        loga_lo = at("loga_lo", S + 37.25, [P, CHUNKS, HEADS], FP32R)
        dec_end = at("dec_end", S + 37.75, [P, HEADS])
        dec_in = at("dec_in", S + 38, [P, HEADS])
        skip_b = at("skip_b", S + 38.25, [P, HEADS])
        b_now = at("b_now", S + 38.5, [P, STATE])
        c_now = at("c_now", S + 39, [P, P])
        seg_hi = at("seg_hi", W, [P, 4, P], FP32R)
        seg_lo = at("seg_lo", W + 2, [P, 4, P], FP32R)
        mix = at("mix", W + 4, [P, 4, 4, P])
        z_act = at("z_act", W + 12, [P, CHUNKS, COLS])

        gate_val = at("gate_val", W, [P, CHUNKS, COLS])
        val = at("val", W + 4, [P, CHUNKS, COLS])
        merged_b = at("merged_b", R, [P, CHUNKS, D_MODEL])
        ya = at("ya", Q, [P, KD, 2, SEQ], FP32R)
        merged = at("merged", Q + 32, [P, KD, 2, SEQ], FP32R)
        a_pre = at("a_pre", Q + 64, [P, TILES, SEQ + CONV_A_K])
        a_conv = at("a_conv", Q + 68.5, [P, TILES, SEQ])
        a_c = at("a_c", Q + 72.5, [P, CHUNKS, COLS])
        a_tok = at("a_tok", Q + 76.5, [P, CHUNKS, COLS])
        a_val = at("a_val", Q + 80.5, [P, TILES, SEQ])
        h_tok = at("h_tok", R, [P, CHUNKS, D_MODEL])
        x_res = at("x_res", Q, [P, CHUNKS, D_MODEL])
        junk = at("junk", W + 8, [P, COLS])
        ff = at("ff", Q, [P, KF, 2, SEQ], FP32R)
        final_b = at("final_b", W + 10, [P, D_MODEL])
        y_out = at("y_out", 48, [P, CHUNKS, D_MODEL])

        ps = ctx.enter_context(nc.psum_tensor("ps", [P, 8, 512], FP32))

        def sem(name):
            return ctx.enter_context(nc.semaphore(name))

        weights_landed = [sem(f"weights_landed{s}") for s in range(SLOTS)]
        weights_hi, weights_split, weights_used = sem("weights_hi"), sem("weights_split"), sem("weights_used")
        x_landed = [sem(f"x_landed{c}") for c in range(CHUNKS)]
        x2_landed = sem("x2_landed")
        rows_landed, heads_landed, dtw_landed = sem("rows_landed"), sem("heads_landed"), sem("dtw_landed")
        final_landed, out_stored = sem("final_landed"), sem("out_stored")
        masks_set, masks_ready, after_ready, pads_zero = sem("masks_set"), sem("masks_ready"), sem("after_ready"), sem("pads_zero")
        params_t, params_ready = sem("params_t"), sem("params_ready")
        nrm_sum, nrm_ms, nrm_rms, nrm_rstd = sem("nrm_sum"), sem("nrm_ms"), sem("nrm_rms"), sem("nrm_rstd")
        nrm_scaled, nrm_t, nrm_hi, nrm_lo = sem("nrm_scaled"), sem("nrm_t"), sem("nrm_hi"), sem("nrm_lo")
        root_ready, zero_set = sem("root_ready"), sem("zero_set")
        dtw_hi_ok, dtw_ready, dt_sums, dt_half_kept, dt_cols_kept, dt_raw = (
            sem("dtw_hi_ok"), sem("dtw_ready"), sem("dt_sums"), sem("dt_half_kept"), sem("dt_cols_kept"), sem("dt_raw"))
        dt_step, dt_exp, heads_exp = sem("dt_step"), sem("dt_exp"), sem("heads_exp")
        cs_ready, decays_ready = sem("cs_ready"), sem("decays_ready")
        acc_copied = sem("acc_copied")
        conv_first, conv_taps, conv_act = sem("conv_first"), sem("conv_taps"), sem("conv_act")
        b_t, b_kept, c_kept, cb_ready, cb_kept = sem("b_t"), sem("b_kept"), sem("c_kept"), sem("cb_ready"), sem("cb_kept")
        now_kept = sem("now_kept")
        z_kept, x_t, xprep = sem("z_kept"), sem("x_t"), sem("xprep")
        seg_in, seg_ready, seg_exp, mix_ready = sem("seg_in"), sem("seg_ready"), sem("seg_exp"), sem("mix_ready")
        y_first, y_second, state_kept, y_sum = sem("y_first"), sem("y_second"), sem("state_kept"), sem("y_sum")
        g_sq, g_ms, g_rms, g_scaled = sem("g_sq"), sem("g_ms"), sem("g_rms"), sem("g_scaled")
        yz_t, yz_hi, yz_lo = sem("yz_t"), sem("yz_hi"), sem("yz_lo")
        g_rstd = sem("g_rstd")
        gate_done, mb_done = sem("gate_done"), sem("mb_done")
        ac_kept, ch_done, a_first, a_taps = sem("ac_kept"), sem("ch_done"), sem("a_first"), sem("a_taps")
        ch_t, a_pre_kept, b_tok_kept, a_b_t = sem("ch_t"), sem("a_pre_kept"), sem("b_tok_kept"), sem("a_b_t")
        a_done, a_hi, a_lo = sem("a_done"), sem("a_hi"), sem("a_lo")
        val_part, val_done, val_t, out_hi, out_lo = (
            sem("val_part"), sem("val_done"), sem("val_t"), sem("out_hi"), sem("out_lo"))
        h_sum, h_sq, h_t, h_hi, h_lo = sem("h_sum"), sem("h_sq"), sem("h_t"), sem("h_hi"), sem("h_lo")
        h_part, h_ms, h_rms, h_rstd = sem("h_part"), sem("h_ms"), sem("h_rms"), sem("h_rstd")
        d_summed, d_sq, d_gained = sem("d_summed"), sem("d_sq"), sem("d_gained")
        d_last = sem("d_last")
        fin_ready = [sem(f"fin_ready{c}") for c in range(CHUNKS)]

        block = ctx.enter_context(nc.Block())

        def blk2(b):
            return ps[:, b:b + 2, :].rearrange("p b (m t) -> p (b m) t", t=SEQ)

        def per_head(ap):
            return ap.unsqueeze(2).to_broadcast([P, HEADS_G, HEAD_DIM])

        def heads_of(ap):
            return ap.rearrange("p (h d) -> p h d", d=HEAD_DIM)

        rows = [ssm_conv_w.rearrange("a k (t p) -> (a k t) p", p=P),
                ssm_conv_b.rearrange("a (t p) -> (a t) p", p=P),
                norm_mix_g.rearrange("a (t p) -> (a t) p", p=P),
                conv_a_w.rearrange("a k (t p) -> (a k t) p", p=P),
                ssm_norm_g.rearrange("a (t p) -> (a t) p", p=P),
                norm_ffn_g.rearrange("a (t p) -> (a t) p", p=P)]
        parameter_loads, at_row = [], 0
        for r in rows:
            done = 0
            while done < r.shape[0]:
                n = min(r.shape[0] - done, P - at_row % P)
                parameter_loads.append((par_rows[at_row % P:at_row % P + n, at_row // P, :], r[done:done + n, :]))
                done += n
                at_row += n

        @block.sync
        def _(sp):
            def load(n, c, w, row0, col):
                s = c % SLOTS
                sp.dma_start(raw[s][:, :, :],
                             w[row0:row0 + KP * P, bass.ds(col, COLS)].rearrange("(k p) n -> p k n", p=P))\
                  .then_inc(weights_landed[s], 16)

            def load_block(n0, w, pieces, col, row_first=0, first=False):
                for c in range(pieces):
                    if first and c == SLOTS:
                        load_dt()
                    if not (first and c < SLOTS):
                        sp.wait_ge(weights_split, n0 + c - (SLOTS - 1))
                    load(n0 + c, c, w, (row_first + c) * KP * P, col)

            x_v = x[0].rearrange("(c p) d -> p c d", p=P)
            for c in range(CHUNKS):
                sp.dma_start(x_tok[:, c, :], x_v[:, c, :]).then_inc(x_landed[c], 16)
            for dst, src in parameter_loads:
                sp.dma_start(dst, src).then_inc(rows_landed, 16)

            def load_dt():
                sp.dma_start(dtw_raw[:, :, :], w_in[0][:, OFF_DT:OFF_DT + HEADS].rearrange("(k p) n -> p k n", p=P))\
                  .then_inc(dtw_landed, 16)
                for dst, src in ((bias_b, dt_bias), (alog_b, a_log), (skip_b, d_skip)):
                    sp.dma_start(dst[:, :], src[0].partition_broadcast(P)).then_inc(heads_landed, 16)

            for i in range(2):
                load_block(N_BC + 2 * i * NP_D, w_in[0], NP_D, OFF_XBC + D_INNER + i * COLS, first=(i == 0))
                load_block(N_BC + (2 * i + 1) * NP_D, w_in[0], NP_D,
                           OFF_XBC + D_INNER + GROUPS * STATE + i * COLS)
            with sp.Fori(0, GROUPS) as g:
                load_block(N_G + g * (2 * NP_D), w_in[0], NP_D, OFF_XBC + g * COLS)
                load_block(N_G + g * (2 * NP_D) + NP_D, w_in[0], NP_D, OFF_Z + g * COLS)
            with sp.Fori(1, BLK_D + 1) as i:
                n = (N_OS - (NP_D + NP_I)) + i * (NP_D + NP_I)
                load_block(n, w_in[0], NP_D, (OFF_GATE_B - COLS) + i * COLS)
                load_block(n + NP_D, w_out_ssm[0], NP_I, i * COLS - COLS)
            with sp.Fori(0, BLK_D) as i:
                for j, part in enumerate((1, 2, 0)):
                    load_block(N_A + i * (3 * NP_D) + j * NP_D, w_in[0], NP_D, OFF_A + part * D_MODEL + i * COLS)
            with sp.Fori(0, BLK_D) as i:
                load_block(N_OA + i * (2 * NP_D), w_in[0], NP_D, OFF_GATE_A + i * COLS)
                load_block(N_OA + i * (2 * NP_D) + NP_D, w_out_a[0], NP_D, i * COLS)
            load_block(N_O, w_o[0], NP_D, 0)
            sp.wait_ge(weights_used, N_O)
            for c in range(CHUNKS):
                sp.dma_start(x_res[:, c, :], x_v[:, c, :]).then_inc(x2_landed, 16)
            sp.dma_start(final_b[:, :], norm_final_g.partition_broadcast(P)).then_inc(final_landed, 16)
            with sp.Fori(1, BLK_D) as i:
                load_block(N_O + i * NP_D, w_o[0], NP_D, i * COLS)
            with sp.Fori(0, BLK_F) as i:
                load_block(N_F + i * (2 * NP_D), w_ffn_gate[0], NP_D, i * COLS)
                load_block(N_F + i * (2 * NP_D) + NP_D, w_ffn_up[0], NP_D, i * COLS)
            with sp.Fori(0, BLK_D // 2) as i:
                for c in range(2 * NP_F):
                    sp.wait_ge(weights_split, N_DN + i * (2 * NP_F) + c - (SLOTS - 1))
                    load(None, c, w_ffn_down[0], (c % NP_F) * KP * P, (2 * i + c // NP_F) * COLS)
            out_v = out[0].rearrange("(c p) d -> p c d", p=P)
            for c in range(CHUNKS):
                sp.wait_ge(fin_ready[c], 2)
                sp.dma_start(out_v[:, c, :], y_out[:, c, :]).then_inc(out_stored, 16)
            sp.wait_ge(out_stored, 16 * CHUNKS)

        @block.gpsimd
        def _(pool):
            nc.gpsimd.memset(zero[:, :], 0.0).then_inc(zero_set, 1)
            nc.gpsimd.memset(ident[:, :], 0.0).then_inc(masks_set, 1)
            nc.gpsimd.memset(upto[:, :], 1.0).then_inc(masks_set, 1)
            nc.gpsimd.memset(after_f[:, :], 1.0).then_inc(masks_set, 1)
            nc.gpsimd.memset(x_pre[:, :, 0:CONV_K - 1], 0.0).then_inc(pads_zero, 1)
            pool.wait_ge(masks_set, 3)
            nc.gpsimd.affine_select(out=ident[:, :], in_=ident[:, :], compare_op=ALU.not_equal, fill=1.0,
                                    base=0, pattern=[[-1, P]], channel_multiplier=1).then_inc(masks_ready, 1)
            nc.gpsimd.affine_select(out=upto[:, :], in_=upto[:, :], compare_op=ALU.is_ge, fill=0.0,
                                    base=0, pattern=[[1, P]], channel_multiplier=-1).then_inc(masks_ready, 1)
            nc.gpsimd.affine_select(out=after_f[:, :], in_=after_f[:, :], compare_op=ALU.is_gt, fill=0.0,
                                    base=0, pattern=[[-1, P]], channel_multiplier=1).then_inc(masks_ready, 1)
            pool.wait_ge(weights_used, N_A)
            nc.gpsimd.memset(a_pre[:, :, 0:CONV_A_K - 1], 0.0).then_inc(pads_zero, 1)

        @block.scalar
        def _(act):
            def hi(n, c):
                s = c % SLOTS
                act.wait_ge(weights_landed[s], (n - s) * (16 // SLOTS) + 16)
                if not (isinstance(n, int) and n < SLOTS):
                    act.wait_ge(weights_used, n - (SLOTS - 1))
                nc.scalar.activation(w_hi[s][:, :, :], raw[s][:, :, :], ACT.Copy).then_inc(weights_hi, 1)

            def stream(n0, pieces, steps):
                for c in range(pieces):
                    hi(n0 + c, c)
                    for f in steps.get(c, []):
                        f()

            def both(a, b):
                return {k: a.get(k, []) + b.get(k, []) for k in sorted(set(a) | set(b))}

            act.wait_ge(zero_set, 1)
            nc.scalar.activation(root[:, :], zero[:, :], ACT.Sqrt).then_inc(root_ready, 1)
            for c in range(CHUNKS):
                act.wait_ge(x_landed[c], 16)
                nc.scalar.activation(x_nrm[:, c, :], x_tok[:, c, :], ACT.Square, accum_out=row_sum[:, c:c + 1])\
                    .then_inc(nrm_sum, 1)
                act.wait_ge(nrm_ms, c + 1)
                nc.scalar.activation(row_rms[:, c:c + 1], row_ms[:, c:c + 1], ACT.Sqrt).then_inc(nrm_rms, 1)

            def norm_hi(b):
                def f():
                    act.wait_ge(params_ready, 1)
                    act.wait_ge(nrm_t, b + 1)
                    for j in range(2):
                        t = 2 * b + j
                        nc.scalar.activation(normed[:, t, 0, :], ps[:, b, j * SEQ:(j + 1) * SEQ], ACT.Copy,
                                             scale=params[:, PC_MIX_G + t:PC_MIX_G + t + 1]).then_inc(nrm_hi, 1)
                return f

            def dt_weights():
                act.wait_ge(dtw_landed, 16)
                nc.scalar.activation(dtw_hi[:, :, :], dtw_raw[:, :, :], ACT.Copy).then_inc(dtw_hi_ok, 1)
                act.wait_ge(heads_landed, 48)
                nc.scalar.activation(anow_b[:, :], alog_b[:, :], ACT.Exp).then_inc(heads_exp, 1)

            def keep_dt_half():
                act.wait_ge(dt_sums, 1)
                nc.scalar.activation(dt_half[:, :], ps[0:HEADS, 7, SEQ:2 * SEQ], ACT.Copy).then_inc(dt_half_kept, 1)

            def dt_exponential():
                act.wait_ge(dt_step, 3)
                nc.scalar.activation(dt_tmp[3][:, :], dt_tmp[2][:, :], ACT.Exp).then_inc(dt_exp, 1)

            def decays():
                act.wait_ge(cs_ready, 1)
                nc.scalar.activation(dec_end[:, :], ps[:, 7, 0:HEADS], ACT.Exp).then_inc(decays_ready, 1)
                nc.scalar.activation(dec_in[:, :], ps[:, 7, HEADS:2 * HEADS], ACT.Exp).then_inc(decays_ready, 1)

            def copy_block(q, used, bank):
                def f():
                    act.wait_ge(weights_used, used)
                    if not (isinstance(q, int) and q == 0):
                        act.wait_ge(conv_taps, q * 12)
                    else:
                        act.wait_ge(pads_zero, 1)
                    nc.scalar.activation(x_pre[:, :, CONV_K - 1:CONV_K - 1 + SEQ], blk2(bank), ACT.Copy)\
                        .then_inc(acc_copied, 1)
                return f

            def conv_first_tap(q, tile):
                def f():
                    act.wait_ge(acc_copied, q + 1)
                    if not (isinstance(q, int) and q == 0):
                        act.wait_ge(conv_act, q)
                    if not isinstance(q, int):
                        act.wait_ge(x_t, 2 * (q - 4))
                    for m in range(TILES):
                        nc.scalar.activation(
                            x_conv[:, m, :], x_pre[:, m, CONV_K - 1:CONV_K - 1 + SEQ], ACT.Identity,
                            scale=params[:, bass.ds(tile + (PC_CONV_W + (CONV_K - 1) * CONV_TILES + m), 1)],
                            bias=params[:, bass.ds(tile + (PC_CONV_B + m), 1)]).then_inc(conv_first, 1)
                return f

            def conv_silu(q, dst):
                def f():
                    act.wait_ge(conv_taps, (q + 1) * 12)
                    if isinstance(q, int) and q in (2, 3):
                        act.wait_ge(cb_ready, 1)
                    nc.scalar.activation(dst[:, :, :], x_conv[:, :, :], ACT.Silu).then_inc(conv_act, 1)
                return f

            def keep_b(i):
                def f():
                    act.wait_ge(b_t, i + 1)
                    nc.scalar.activation(b_first[:, TILES * i:TILES * (i + 1), :].rearrange("p g n -> p (g n)"),
                                         ps[:, 6, :], ACT.Copy).then_inc(b_kept, 1)
                return f

            def keep_c(i):
                def f():
                    act.wait_ge(conv_act, 2 * i + 2)
                    nc.scalar.activation(c_last[:, TILES * i:TILES * (i + 1), :], c_feat[:, :, P:2 * P],
                                         ACT.Copy).then_inc(c_kept, 1)
                return f

            B_TILE, C_TILE = D_INNER // P, D_INNER // P + GROUPS

            def c_steps(i):
                n = N_BC + (2 * i + 2) * NP_D
                return {1: [keep_b(i)], 2: [copy_block(2 * i + 1, n, 4)],
                        3: [conv_first_tap(2 * i + 1, C_TILE + TILES * i)],
                        7: [conv_silu(2 * i + 1, c_feat), keep_c(i)]}

            for i in range(2):
                n = N_BC + 2 * i * NP_D
                steps = {9: [copy_block(2 * i, n + NP_D, 0)],
                         10: [conv_first_tap(2 * i, B_TILE + TILES * i)],
                         13: [conv_silu(2 * i, b_feat)]}
                if i == 0:
                    steps |= {c: [norm_hi(0), norm_hi(1)] if c == 0 else [norm_hi(c + 1)] for c in range(7)}
                    steps = both(steps, {6: [dt_weights], 10: [keep_dt_half], 14: [dt_exponential]})
                else:
                    steps = both(steps, both(c_steps(0), {3: [decays]}))
                stream(n, 2 * NP_D, steps)

            def now(g):
                def f():
                    act.wait_ge(c_kept, 2)
                    act.wait_ge(b_kept, 2)
                    if not (isinstance(g, int) and g == 0):
                        act.wait_ge(y_second, g)
                    nc.scalar.activation(b_now[:, :], b_first[:, bass.ds(g, 1), :].rearrange("p a n -> p (a n)"),
                                         ACT.Copy).then_inc(now_kept, 1)
                    nc.scalar.activation(c_now[:, :], c_last[:, bass.ds(g, 1), :].rearrange("p a n -> p (a n)"),
                                         ACT.Copy).then_inc(now_kept, 1)
                return f

            def keep_z(g, used):
                def f():
                    act.wait_ge(weights_used, used)
                    if not (isinstance(g, int) and g == 0):
                        act.wait_ge(g_sq, 2 * g)
                    nc.scalar.activation(z_act[:, :, :], ps[:, 4:6, :], ACT.Silu).then_inc(z_kept, 1)
                return f

            def seg_exponential(g, b):
                def f():
                    act.wait_ge(seg_ready, 4 * g + b + 1)
                    if not (isinstance(g, int) and g == 0):
                        act.wait_ge(y_first if b < 2 else y_second, g)
                    nc.scalar.activation(mix[:, b, :, :].rearrange("p h l -> p (h l)"), ps[:, 2 + b % 2, :],
                                         ACT.Exp).then_inc(seg_exp, 1)
                return f

            def keep_state(g):
                def f():
                    act.wait_ge(y_first, g + 1)
                    if not (isinstance(g, int) and g == 0):
                        act.wait_ge(y_second, g)
                    nc.scalar.activation(state_sb[:, :], ps[:, 6, :], ACT.Copy).then_inc(state_kept, 1)
                return f

            def group_squares(g):
                def f():
                    for c in range(CHUNKS):
                        act.wait_ge(y_sum, 6 * g + 6)
                        nc.scalar.activation(z_act[:, c, :], y[:, c, :], ACT.Square,
                                             accum_out=grp_sum[:, c:c + 1]).then_inc(g_sq, 1)
                return f

            def group_root(g):
                def f():
                    act.wait_ge(g_ms, g + 1)
                    nc.scalar.activation(grp_rms[:, :], grp_ms[:, :], ACT.Sqrt).then_inc(g_rms, 1)
                return f

            def keep_yz_hi(g):
                def f():
                    for m in range(TILES):
                        act.wait_ge(yz_t, 2 * g + m // 2 + 1)
                        nc.scalar.activation(
                            yz[:, bass.ds(TILES * g + m, 1), 0, :].rearrange("p a t -> p (a t)"),
                            ps[:, 6 + m // 2, (m % 2) * SEQ:(m % 2 + 1) * SEQ],
                            ACT.Copy, scale=params[:, bass.ds(TILES * g + (PC_SSM_G + m), 1)]).then_inc(yz_hi, 1)
                return f

            def own_steps(g):
                n = N_G + g * (2 * NP_D)
                return {5: [seg_exponential(g, 0)], 8: [seg_exponential(g, 1)], 11: [seg_exponential(g, 2)],
                        13: [seg_exponential(g, 3)],
                        9: [copy_block(g + 4, n + NP_D, 0)],
                        10: [conv_first_tap(g + 4, g * TILES)],
                        14: [conv_silu(g + 4, x_conv)]}

            def last_steps(g):
                n = N_G + g * (2 * NP_D)
                return {1: [now(g)], 2: [keep_z(g, n + 2 * NP_D)], 5: [keep_state(g)], 9: [group_squares(g)],
                        10: [group_root(g)], 14: [keep_yz_hi(g)]}

            stream(N_G, 2 * NP_D, both(c_steps(1), own_steps(0)))
            with act.Fori(0, GROUPS - 1) as g:
                stream((N_G + 2 * NP_D) + g * (2 * NP_D), 2 * NP_D, both(last_steps(g), own_steps(g + 1)))

            def gate(func, used, n_freed, freed, scale=None):
                def f():
                    act.wait_ge(weights_used, used)
                    if n_freed is not None:
                        act.wait_ge(freed, n_freed)
                    if scale is None:
                        nc.scalar.activation(gate_val[:, :, :], ps[:, 0:2, :], func).then_inc(gate_done, 1)
                        return
                    act.wait_ge(h_rstd, 1)
                    for t in range(CHUNKS):
                        ins = nc.scalar.activation(gate_val[:, t, :], ps[:, t, :], func, scale=scale[:, t:t + 1])
                    ins.then_inc(gate_done, 1)
                return f

            def keep_hi(dst, i, v):
                def f():
                    act.wait_ge(val_t, v + 1)
                    nc.scalar.activation(dst[:, bass.ds(TILES * i, TILES), 0, :], blk2(4), ACT.Copy)\
                        .then_inc(out_hi, 1)
                return f

            def os_own(i, first=False):
                n = N_OS + i * (NP_D + NP_I)
                return {10: [gate(ACT.Sigmoid, n + NP_D, None if first else i, mb_done)]}

            stream(N_OS, NP_D + NP_I, both(last_steps(GROUPS - 1), os_own(0, True)))
            with act.Fori(0, BLK_D - 1) as i:
                stream((N_OS + NP_D + NP_I) + i * (NP_D + NP_I), NP_D + NP_I, os_own(i + 1))

            def keep_c_part(i, first):
                def f():
                    act.wait_ge(weights_used, N_A + NP_D + i * (3 * NP_D))
                    if not first:
                        act.wait_ge(ch_done, i)
                    nc.scalar.activation(a_c[:, :, :], ps[:, 0:2, :], ACT.Copy).then_inc(ac_kept, 1)
                return f

            def a_first_tap(i, first):
                def f():
                    act.wait_ge(ch_t, i + 1)
                    if first:
                        act.wait_ge(pads_zero, 2)
                    else:
                        act.wait_ge(a_taps, 8 * i)
                    nc.scalar.activation(a_pre[:, :, CONV_A_K - 1:CONV_A_K - 1 + SEQ], blk2(6), ACT.Copy)\
                        .then_inc(a_pre_kept, 1)
                    act.wait_ge(a_pre_kept, i + 1)
                    if not first:
                        act.wait_ge(a_done, i)
                    for m in range(TILES):
                        nc.scalar.activation(
                            a_conv[:, m, :], a_pre[:, m, CONV_A_K - 1:CONV_A_K - 1 + SEQ], ACT.Copy,
                            scale=params[:, bass.ds(TILES * i + (PC_CONV_A + (CONV_A_K - 1) * KD + m), 1)])\
                            .then_inc(a_first, 1)
                return f

            def keep_b_part(i):
                def f():
                    act.wait_ge(weights_used, N_A + 3 * NP_D + i * (3 * NP_D))
                    act.wait_ge(ch_t, i + 1)
                    nc.scalar.activation(a_tok[:, :, :], ps[:, 4:6, :], ACT.Copy).then_inc(b_tok_kept, 1)
                return f

            def keep_a_hi(i):
                def f():
                    act.wait_ge(a_done, i + 1)
                    nc.scalar.activation(ya[:, bass.ds(TILES * i, TILES), 0, :], a_val[:, :, :], ACT.Copy)\
                        .then_inc(a_hi, 1)
                return f

            def a_own(i, first=False):
                return {10: [keep_c_part(i, first)], 22: [a_first_tap(i, first)]}

            def a_last(i):
                return {2: [keep_b_part(i)], 7: [keep_a_hi(i)]}

            stream(N_A, 3 * NP_D, a_own(0, True))
            with act.Fori(0, BLK_D - 1) as i:
                stream((N_A + 3 * NP_D) + i * (3 * NP_D), 3 * NP_D, both(a_last(i), a_own(i + 1)))

            def oa_own(i, first=False):
                n = N_OA + i * (2 * NP_D)
                freed = (BLK_D, mb_done) if first else (i, val_part)
                return {10: [gate(ACT.Sigmoid, n + NP_D, *freed)]}

            stream(N_OA, 2 * NP_D, both(a_last(BLK_D - 1), oa_own(0, True)))
            with act.Fori(0, BLK_D - 1) as i:
                stream((N_OA + 2 * NP_D) + i * (2 * NP_D), 2 * NP_D,
                       both({5: [keep_hi(merged, i, i)]}, oa_own(i + 1)))

            def h_squares(c):
                def f():
                    for t in range(CHUNKS):
                        act.wait_ge(h_sum, 2 * c + t + 1)
                        if not (isinstance(c, int) and c == 0 and t == 0):
                            act.wait_ge(h_sq, 2 * c + t)
                        nc.scalar.activation(junk[:, :], h_tok[:, t, bass.ds(c * COLS, COLS)], ACT.Square,
                                             accum_out=row_part[:, t, bass.ds(c, 1)]).then_inc(h_sq, 1)
                return f

            def keep_h_hi(c):
                def f():
                    for m in range(TILES):
                        act.wait_ge(h_t, 2 * c + m // 2 + 1)
                        nc.scalar.activation(
                            normed[:, bass.ds(TILES * c + m, 1), 0, :].rearrange("p a t -> p (a t)"),
                            ps[:, 6 + m // 2, (m % 2) * SEQ:(m % 2 + 1) * SEQ], ACT.Copy,
                            scale=params[:, bass.ds(TILES * c + (PC_FFN_G + m), 1)]).then_inc(h_hi, 1)
                return f

            def o_last(c):
                return {3: [h_squares(c)], 5: [keep_h_hi(c)]}

            stream(N_O, NP_D, {5: [keep_hi(merged, BLK_D - 1, BLK_D - 1)]})
            with act.Fori(0, BLK_D - 1) as c:
                stream((N_O + NP_D) + c * NP_D, NP_D, o_last(c))

            def h_root():
                act.wait_ge(h_ms, 1)
                nc.scalar.activation(row_rms[:, :], row_ms[:, :], ACT.Sqrt).then_inc(h_rms, 1)

            def f_own(i, first=False):
                n = N_F + i * (2 * NP_D)
                freed = (BLK_D, val_part) if first else (i + BLK_D, val_done)
                return {10: [gate(ACT.Silu, n + NP_D, *freed, scale=row_rstd)]}

            stream(N_F, 2 * NP_D, both(both(o_last(BLK_D - 1), {8: [h_root]}), f_own(0, True)))
            with act.Fori(0, BLK_F - 1) as i:
                stream((N_F + 2 * NP_D) + i * (2 * NP_D), 2 * NP_D,
                       both({5: [keep_hi(ff, i, i + BLK_D)]}, f_own(i + 1)))

            def d_squares(c):
                def f():
                    for t in range(CHUNKS):
                        square_h(c, t)
                return f

            def square_h(c, t):
                act.wait_ge(d_summed, 2 * c + t + 1)
                act.wait_ge(h_sq, 2 * BLK_D)
                if c or t:
                    act.wait_ge(d_sq, 2 * c + t)
                nc.scalar.activation(junk[:, :], h_tok[:, t, c * COLS:(c + 1) * COLS], ACT.Square,
                                     accum_out=row_part[:, t, c:c + 1]).then_inc(d_sq, 1)

            stream(N_DN, 2 * NP_F, {5: [keep_hi(ff, BLK_F - 1, BLK_D + BLK_F - 1)], NP_F + 3: [d_squares(0)]})
            stream(N_DN + 2 * NP_F, 2 * NP_F, {3: [d_squares(1)], NP_F + 3: [d_squares(2)]})
            nc.scalar.activation(root[:, :], zero[:, :], ACT.Sqrt)
            for t in range(CHUNKS):
                square_h(BLK_D - 1, t)
                act.wait_ge(h_ms, t + 2)
                nc.scalar.activation(row_rms[:, t:t + 1], row_ms[:, t:t + 1], ACT.Sqrt).then_inc(h_rms, 1)
                act.wait_ge(h_rstd, t + 2)
                act.wait_ge(d_gained, 2 * (BLK_D - 1) + t + 1)
                nc.scalar.activation(y_out[:, t, DVE_COLS:], y_out[:, t, DVE_COLS:], ACT.Copy, scale=row_rstd[:, t:t + 1])\
                    .then_inc(fin_ready[t], 1)

        @block.vector
        def _(dve):
            def lo(n, c):
                s = c % SLOTS
                dve.wait_ge(weights_hi, n + 1)
                nc.vector.tensor_tensor(w_lo[s][:, :, :], raw[s][:, :, :], w_hi[s][:, :, :].bitcast(FP32),
                                        ALU.subtract).then_inc(weights_split, 1)

            def stream(n0, pieces, steps):
                for c in range(pieces):
                    lo(n0 + c, c)
                    for f in steps.get(c, []):
                        f()

            def both(a, b):
                return {k: a.get(k, []) + b.get(k, []) for k in sorted(set(a) | set(b))}

            dve.wait_ge(masks_ready, 3)
            nc.vector.tensor_copy(after[:, :], after_f[:, :]).then_inc(after_ready, 1)
            for c in range(CHUNKS):
                dve.wait_ge(nrm_sum, c + 1)
                nc.vector.tensor_scalar(row_ms[:, c:c + 1], row_sum[:, c:c + 1], 1.0 / D_MODEL, EPS, ALU.mult, ALU.add)\
                    .then_inc(nrm_ms, 1)
                dve.wait_ge(nrm_rms, c + 1)
                nc.vector.reciprocal(row_rstd[:, c:c + 1], row_rms[:, c:c + 1]).then_inc(nrm_rstd, 1)
                dve.wait_ge(nrm_rstd, c + 1)
                nc.vector.tensor_scalar(x_nrm[:, c, :], x_tok[:, c, :], row_rstd[:, c:c + 1], None, ALU.mult)\
                    .then_inc(nrm_scaled, 1)
            dve.wait_ge(params_t, 1)
            nc.vector.tensor_copy(params[:, :], ps[:, 7, 0:PC_ALL]).then_inc(params_ready, 1)
            dve.wait_ge(params_ready, 1)

            def norm_lo(b):
                def f():
                    dve.wait_ge(nrm_hi, 2 * b + 2)
                    for j in range(2):
                        t = 2 * b + j
                        nc.vector.scalar_tensor_tensor(
                            out=normed[:, t, 1, :], in0=ps[:, b, j * SEQ:(j + 1) * SEQ],
                            scalar=params[:, PC_MIX_G + t:PC_MIX_G + t + 1], in1=normed[:, t, 0, :].bitcast(FP32),
                            op0=ALU.mult, op1=ALU.subtract).then_inc(nrm_lo, 1)
                return f

            def dt_weights():
                dve.wait_ge(dtw_hi_ok, 1)
                nc.vector.tensor_tensor(dtw_lo[:, :, :], dtw_raw[:, :, :], dtw_hi[:, :, :].bitcast(FP32),
                                        ALU.subtract).then_inc(dtw_ready, 1)

            def keep_dt_cols():
                dve.wait_ge(dt_half_kept, 1)
                nc.vector.tensor_tensor(dt_cols[:, :], ps[0:HEADS, 7, 0:SEQ], dt_half[:, :], ALU.add)\
                    .then_inc(dt_cols_kept, 1)

            def dt_link(ins):
                ins.then_inc(dt_step, 1)
                dt_link.count += 1
                dve.wait_ge(dt_step, dt_link.count)
            dt_link.count = 0
            v, neg, nabs, a, den, rec, z, z2, p, pos = dt_tmp

            def by_chunk(ap):
                return ap.rearrange("p (c h) -> p c h", c=CHUNKS)

            def over_chunks(ap):
                return ap.unsqueeze(1).to_broadcast([P, CHUNKS, HEADS])

            def dt_argument():
                dve.wait_ge(dt_raw, 1)
                dve.wait_ge(heads_landed, 48)
                dt_link(nc.vector.tensor_tensor(by_chunk(v[:, :]), by_chunk(ps[:, 6, 0:CHUNKS * HEADS]),
                                                over_chunks(bias_b[:, :]), ALU.add))
                dt_link(nc.vector.tensor_scalar(neg[:, :], v[:, :], -1.0, None, ALU.mult))
                dt_link(nc.vector.tensor_tensor(nabs[:, :], v[:, :], neg[:, :], ALU.min))

            def dt_rest():
                dve.wait_ge(dt_exp, 1)
                dt_link(nc.vector.tensor_scalar(den[:, :], a[:, :], 2.0, None, ALU.add))
                dt_link(nc.vector.reciprocal(rec[:, :], den[:, :]))
                dt_link(nc.vector.tensor_tensor(z[:, :], a[:, :], rec[:, :], ALU.mult))
                dt_link(nc.vector.tensor_tensor(z2[:, :], z[:, :], z[:, :], ALU.mult))
                dt_link(nc.vector.tensor_scalar(p[:, :], z2[:, :], 1.0 / 19, None, ALU.mult))
                for odd in range(17, 1, -2):
                    dt_link(nc.vector.scalar_tensor_tensor(out=p[:, :], in0=p[:, :], scalar=1.0 / odd,
                                                           in1=z2[:, :], op0=ALU.add, op1=ALU.mult))
                dt_link(nc.vector.scalar_tensor_tensor(out=p[:, :], in0=p[:, :], scalar=1.0, in1=z[:, :],
                                                       op0=ALU.add, op1=ALU.mult))
                dt_link(nc.vector.tensor_scalar(pos[:, :], v[:, :], 0.0, None, ALU.max))
                dt_link(nc.vector.scalar_tensor_tensor(
                    out=dt[:, :, :].rearrange("p c h -> p (c h)"), in0=p[:, :], scalar=2.0, in1=pos[:, :],
                    op0=ALU.mult, op1=ALU.add))
                dve.wait_ge(heads_exp, 1)
                dt_link(nc.vector.scalar_tensor_tensor(out=loga[:, :, :], in0=dt[:, :, :], scalar=-1.0,
                                                       in1=over_chunks(anow_b[:, :]), op0=ALU.mult, op1=ALU.mult))
                dt_link(nc.vector.tensor_copy(loga_hi[:, :, :], loga[:, :, :]))
                dt_link(nc.vector.tensor_tensor(loga_lo[:, :, :], loga[:, :, :],
                                                loga_hi[:, :, :].bitcast(FP32), ALU.subtract))

            def conv_tap(q, tile, j):
                def f():
                    before = 12 * q + 4 * (CONV_K - 2 - j)
                    for m in range(TILES):
                        if j == CONV_K - 2:
                            dve.wait_ge(conv_first, 4 * q + m + 1)
                        else:
                            dve.wait_ge(conv_taps, before - 4 + m + 1)
                        nc.vector.scalar_tensor_tensor(
                            out=x_conv[:, m, :], in0=x_pre[:, m, j:j + SEQ],
                            scalar=params[:, bass.ds(tile + (PC_CONV_W + j * CONV_TILES + m), 1)],
                            in1=x_conv[:, m, :], op0=ALU.mult, op1=ALU.add).then_inc(conv_taps, 1)
                return f

            def keep_cb(i):
                def f():
                    dve.wait_ge(cb_ready, i + 1)
                    for c in range(CHUNKS):
                        nc.vector.tensor_tensor(cb[:, TILES * i:TILES * (i + 1), c, :],
                                                ps[:, 6 + c, :].rearrange("p (g l) -> p g l", l=P),
                                                upto[:, :].unsqueeze(1).to_broadcast([P, TILES, P]), ALU.mult)\
                            .then_inc(cb_kept, 1)
                return f

            B_TILE, C_TILE = D_INNER // P, D_INNER // P + GROUPS

            def conv_steps(q, tile, s):
                return {s: [conv_tap(q, tile, 2)], s + 1: [conv_tap(q, tile, 1)], s + 2: [conv_tap(q, tile, 0)]}

            def c_steps(i):
                return both(conv_steps(2 * i + 1, C_TILE + TILES * i, 3), {13 if i else 11: [keep_cb(i)]})

            for i in range(2):
                steps = conv_steps(2 * i, B_TILE + TILES * i, 10)
                if i == 0:
                    steps = both(steps, {c: [norm_lo(0), norm_lo(1)] if c == 0 else [norm_lo(c + 1)]
                                         for c in range(7)})
                    steps = both(steps, {6: [dt_weights], 10: [keep_dt_cols], 13: [dt_argument], 15: [dt_rest]})
                else:
                    steps = both(steps, c_steps(0))
                stream(N_BC + 2 * i * NP_D, 2 * NP_D, steps)

            def seg_input(g, b):
                c, h = b // 2, HEADS_G * g + 4 * (b % 2)
                def f():
                    if not (isinstance(g, int) and g == 0 and b == 0):
                        dve.wait_ge(seg_ready, 4 * g + b)
                    else:
                        dve.wait_ge(dt_step, dt_link.count)
                    for dst, src in ((seg_hi, loga_hi), (seg_lo, loga_lo)):
                        nc.vector.tensor_tensor(
                            dst[:, :, :], upto[:, :].unsqueeze(1).to_broadcast([P, 4, P]),
                            src[:, c, bass.ds(h, 4)].bitcast(FP32).unsqueeze(2).to_broadcast([P, 4, P]), ALU.mult)\
                            .then_inc(seg_in, 1)
                return f

            def seg_mix(g, b):
                def f():
                    dve.wait_ge(seg_exp, 4 * g + b + 1)
                    nc.vector.tensor_tensor(
                        mix[:, b, :, :], mix[:, b, :, :],
                        cb[:, bass.ds(g, 1), b // 2, :].to_broadcast([P, 4, P]), ALU.mult).then_inc(mix_ready, 1)
                return f

            def prepare_x(g):
                def f():
                    dve.wait_ge(x_t, 2 * g + 2)
                    dve.wait_ge(decays_ready, 2)
                    if not (isinstance(g, int) and g == 0):
                        dve.wait_ge(yz_t, 2 * g)
                    for c in range(CHUNKS):
                        nc.vector.tensor_tensor(heads_of(y[:, c, :]), heads_of(ps[:, 6 + c, :]),
                                                per_head(skip_b[:, bass.ds(HEADS_G * g, HEADS_G)]), ALU.mult)\
                            .then_inc(xprep, 1)
                        nc.vector.tensor_tensor(heads_of(xdt[:, c, :]), heads_of(ps[:, 6 + c, :]),
                                                per_head(dt[:, c, bass.ds(HEADS_G * g, HEADS_G)]), ALU.mult)\
                            .then_inc(xprep, 1)
                    dve.wait_ge(xprep, 5 * g + 4)
                    nc.vector.tensor_tensor(heads_of(xdec[:, :]), heads_of(xdt[:, 0, :]),
                                            per_head(dec_end[:, bass.ds(HEADS_G * g, HEADS_G)]), ALU.mult)\
                        .then_inc(xprep, 1)
                return f

            def sum_first(g):
                def f():
                    dve.wait_ge(y_first, g + 1)
                    nc.vector.tensor_tensor(y[:, 0, :], y[:, 0, :], ps[:, 7, :], ALU.add).then_inc(y_sum, 1)
                return f

            def sum_second(g):
                def f():
                    dve.wait_ge(y_second, g + 1)
                    nc.vector.tensor_tensor(heads_of(xdec[:, :]), heads_of(ps[:, 6, :]),
                                            per_head(dec_in[:, bass.ds(HEADS_G * g, HEADS_G)]), ALU.mult)\
                        .then_inc(y_sum, 1)
                    nc.vector.tensor_tensor(y[:, 1, :], y[:, 1, :], ps[:, 7, :], ALU.add).then_inc(y_sum, 1)
                    dve.wait_ge(z_kept, g + 1)
                    dve.wait_ge(y_sum, 6 * g + 1)
                    nc.vector.tensor_tensor(y[:, 0, :], y[:, 0, :], z_act[:, 0, :], ALU.mult).then_inc(y_sum, 1)
                    dve.wait_ge(y_sum, 6 * g + 3)
                    nc.vector.tensor_tensor(y[:, 1, :], y[:, 1, :], xdec[:, :], ALU.add).then_inc(y_sum, 1)
                    dve.wait_ge(y_sum, 6 * g + 5)
                    nc.vector.tensor_tensor(y[:, 1, :], y[:, 1, :], z_act[:, 1, :], ALU.mult).then_inc(y_sum, 1)
                return f

            def group_mean(g):
                def f():
                    dve.wait_ge(g_sq, 2 * g + 2)
                    nc.vector.tensor_scalar(grp_ms[:, :], grp_sum[:, :], 1.0 / COLS, EPS, ALU.mult, ALU.add)\
                        .then_inc(g_ms, 1)
                return f

            def group_scale(g):
                def f():
                    dve.wait_ge(g_rms, g + 1)
                    nc.vector.reciprocal(grp_rstd[:, :], grp_rms[:, :]).then_inc(g_rstd, 1)
                    dve.wait_ge(g_rstd, g + 1)
                    for c in range(CHUNKS):
                        nc.vector.tensor_scalar(y[:, c, :], y[:, c, :], grp_rstd[:, c:c + 1], None, ALU.mult)\
                            .then_inc(g_scaled, 1)
                return f

            def keep_yz_lo(g):
                def f():
                    for m in range(TILES):
                        dve.wait_ge(yz_hi, 4 * g + 2 * (m // 2) + 2)
                        nc.vector.scalar_tensor_tensor(
                            out=yz[:, bass.ds(TILES * g + m, 1), 1, :].rearrange("p a t -> p (a t)"),
                            in0=ps[:, 6 + m // 2, (m % 2) * SEQ:(m % 2 + 1) * SEQ],
                            scalar=params[:, bass.ds(TILES * g + (PC_SSM_G + m), 1)],
                            in1=yz[:, bass.ds(TILES * g + m, 1), 0, :].rearrange("p a t -> p (a t)").bitcast(FP32),
                            op0=ALU.mult, op1=ALU.subtract).then_inc(yz_lo, 1)
                return f

            def own_steps(g):
                seg = {s: [seg_input(g, b)] for b, s in enumerate((2, 5, 8, 10))}
                mixes = {s: [seg_mix(g, b)] for b, s in enumerate((5, 8, 11, 14))}
                return both(both(mixes, seg), conv_steps(g + 4, g * TILES, 10))

            def last_steps(g):
                return {1: [prepare_x(g)], 5: [sum_first(g)], 8: [sum_second(g)], 9: [group_mean(g)],
                        10: [group_scale(g)], 14: [keep_yz_lo(g)]}

            stream(N_G, 2 * NP_D, both(c_steps(1), own_steps(0)))
            with dve.Fori(0, GROUPS - 1) as g:
                stream((N_G + 2 * NP_D) + g * (2 * NP_D), 2 * NP_D, both(last_steps(g), own_steps(g + 1)))

            def keep_lo(dst, i, v):
                def f():
                    dve.wait_ge(out_hi, v + 1)
                    nc.vector.tensor_tensor(dst[:, bass.ds(TILES * i, TILES), 1, :], blk2(4),
                                            dst[:, bass.ds(TILES * i, TILES), 0, :].bitcast(FP32), ALU.subtract)\
                        .then_inc(out_lo, 1)
                return f

            def keep_merged_b(i):
                def f():
                    dve.wait_ge(weights_used, N_OS + (NP_D + NP_I) + i * (NP_D + NP_I))
                    dve.wait_ge(gate_done, i + 1)
                    nc.vector.tensor_tensor(merged_b[:, :, bass.ds(COLS * i, COLS)], ps[:, 2:4, :],
                                            gate_val[:, :, :], ALU.mult).then_inc(mb_done, 1)
                return f

            stream(N_OS, NP_D + NP_I, last_steps(GROUPS - 1))
            with dve.Fori(0, BLK_D - 1) as i:
                stream((N_OS + NP_D + NP_I) + i * (NP_D + NP_I), NP_D + NP_I, {2: [keep_merged_b(i)]})

            def product_ch(i, first):
                def f():
                    dve.wait_ge(weights_used, N_A + 2 * NP_D + i * (3 * NP_D))
                    dve.wait_ge(ac_kept, i + 1)
                    if not first:
                        dve.wait_ge(a_b_t, i)
                    nc.vector.tensor_tensor(a_tok[:, :, :], ps[:, 2:4, :], a_c[:, :, :], ALU.mult).then_inc(ch_done, 1)
                return f

            def a_tap(i, j):
                def f():
                    for m in range(TILES):
                        if j == CONV_A_K - 2:
                            dve.wait_ge(a_first, 4 * i + m + 1)
                        else:
                            dve.wait_ge(a_taps, 8 * i + m + 1)
                        nc.vector.scalar_tensor_tensor(
                            out=a_conv[:, m, :], in0=a_pre[:, m, j:j + SEQ],
                            scalar=params[:, bass.ds(TILES * i + (PC_CONV_A + j * KD + m), 1)],
                            in1=a_conv[:, m, :], op0=ALU.mult, op1=ALU.add).then_inc(a_taps, 1)
                return f

            def product_a(i, first):
                def f():
                    dve.wait_ge(a_b_t, i + 1)
                    dve.wait_ge(a_taps, 8 * i + 8)
                    if not first:
                        dve.wait_ge(a_lo, i)
                        dve.wait_ge(a_hi, i)
                    nc.vector.tensor_tensor(a_val[:, :, :], blk2(6), a_conv[:, :, :], ALU.mult).then_inc(a_done, 1)
                return f

            def keep_a_lo(i):
                def f():
                    dve.wait_ge(a_hi, i + 1)
                    nc.vector.tensor_tensor(ya[:, bass.ds(TILES * i, TILES), 1, :], a_val[:, :, :],
                                            ya[:, bass.ds(TILES * i, TILES), 0, :].bitcast(FP32), ALU.subtract)\
                        .then_inc(a_lo, 1)
                return f

            def a_own(i, first=False):
                return {18: [product_ch(i, first)]}

            def a_last(i, first=False):
                return {0: [a_tap(i, 1)], 1: [a_tap(i, 0)], 6: [product_a(i, first)], 7: [keep_a_lo(i)]}

            stream(N_A, 3 * NP_D, both({2: [keep_merged_b(BLK_D - 1)]}, a_own(0, True)))
            stream(N_A + 3 * NP_D, 3 * NP_D, both(a_last(0, True), a_own(1)))
            with dve.Fori(0, BLK_D - 2) as i:
                stream((N_A + 6 * NP_D) + i * (3 * NP_D), 3 * NP_D, both(a_last(i + 1), a_own(i + 2)))

            def oa_value(i, first):
                def f():
                    dve.wait_ge(weights_used, N_OA + 2 * NP_D + i * (2 * NP_D))
                    dve.wait_ge(gate_done, i + (BLK_D + 1))
                    if not first:
                        dve.wait_ge(val_t, i)
                    nc.vector.tensor_tensor(val[:, :, :], ps[:, 2:4, :], gate_val[:, :, :], ALU.mult)\
                        .then_inc(val_part, 1)
                    dve.wait_ge(val_part, i + 1)
                    nc.vector.tensor_tensor(val[:, :, :], val[:, :, :], merged_b[:, :, bass.ds(COLS * i, COLS)],
                                            ALU.add).then_inc(val_done, 1)
                return f

            def oa_last(i, first=False):
                return {2: [oa_value(i, first)], 5: [keep_lo(merged, i, i)]}

            stream(N_OA, 2 * NP_D, a_last(BLK_D - 1))
            stream(N_OA + 2 * NP_D, 2 * NP_D, oa_last(0, True))
            with dve.Fori(0, BLK_D - 2) as i:
                stream((N_OA + 4 * NP_D) + i * (2 * NP_D), 2 * NP_D, oa_last(i + 1))

            def sum_h(c):
                def f():
                    dve.wait_ge(weights_used, N_O + NP_D + c * NP_D)
                    dve.wait_ge(x2_landed, 16 * CHUNKS)
                    bank = 2 * (c % 2) if isinstance(c, int) else None
                    for t in range(CHUNKS):
                        nc.vector.tensor_tensor(h_tok[:, t, bass.ds(c * COLS, COLS)], ps[:, bank + t, :],
                                                x_res[:, t, bass.ds(c * COLS, COLS)], ALU.add).then_inc(h_sum, 1)
                return f

            def keep_h_lo(c):
                def f():
                    for m in range(TILES):
                        dve.wait_ge(h_hi, 4 * c + 2 * (m // 2) + 2)
                        nc.vector.scalar_tensor_tensor(
                            out=normed[:, TILES * c + m, 1, :],
                            in0=ps[:, 6 + m // 2, (m % 2) * SEQ:(m % 2 + 1) * SEQ],
                            scalar=params[:, PC_FFN_G + TILES * c + m:PC_FFN_G + TILES * c + m + 1],
                            in1=normed[:, TILES * c + m, 0, :].bitcast(FP32),
                            op0=ALU.mult, op1=ALU.subtract).then_inc(h_lo, 1)
                return f

            def o_last(c):
                return {2: [sum_h(c)], 5: [keep_h_lo(c)]}

            stream(N_O, NP_D, oa_last(BLK_D - 1))
            for c in range(BLK_D - 1):
                stream(N_O + (c + 1) * NP_D, NP_D, o_last(c))

            def mean_square(sq, n_sq, k, t0=0, t1=CHUNKS):
                dve.wait_ge(sq, n_sq)
                nc.vector.reduce_sum(row_sum[:, t0:t1], row_part[:, t0:t1, :], axis=mybir.AxisListType.X)\
                    .then_inc(h_part, 1)
                dve.wait_ge(h_part, k + 1)
                nc.vector.tensor_scalar(row_ms[:, t0:t1], row_sum[:, t0:t1], 1.0 / D_MODEL, EPS, ALU.mult, ALU.add)\
                    .then_inc(h_ms, 1)

            def reciprocal_root(k, t0=0, t1=CHUNKS):
                dve.wait_ge(h_rms, k + 1)
                nc.vector.reciprocal(row_rstd[:, t0:t1], row_rms[:, t0:t1]).then_inc(h_rstd, 1)

            def f_value(i):
                def f():
                    dve.wait_ge(weights_used, N_F + 2 * NP_D + i * (2 * NP_D))
                    dve.wait_ge(gate_done, i + (2 * BLK_D + 1))
                    dve.wait_ge(val_t, i + BLK_D)
                    for t in range(CHUNKS):
                        ins = nc.vector.scalar_tensor_tensor(
                            out=val[:, t, :], in0=ps[:, 2 + t, :], scalar=row_rstd[:, t:t + 1],
                            in1=gate_val[:, t, :], op0=ALU.mult, op1=ALU.mult)
                    ins.then_inc(val_done, 1)
                return f

            def f_last(i):
                return {2: [f_value(i)], 5: [keep_lo(ff, i, i + BLK_D)]}

            stream(N_F, 2 * NP_D, both(o_last(BLK_D - 1), {7: [lambda: mean_square(h_sq, 2 * BLK_D, 0)],
                                                           8: [lambda: reciprocal_root(0)]}))
            with dve.Fori(0, BLK_F - 1) as i:
                stream((N_F + 2 * NP_D) + i * (2 * NP_D), 2 * NP_D, f_last(i))

            def sum_down(c):
                def f():
                    dve.wait_ge(weights_used, N_DN + (c + 1) * NP_F)
                    for t in range(CHUNKS):
                        add_down(c, t)
                return f

            def add_down(c, t):
                part = h_tok[:, t, c * COLS:(c + 1) * COLS]
                nc.vector.tensor_tensor(part, part, ps[:, 2 * (c % 2) + t, :], ALU.add).then_inc(d_summed, 1)

            def gain_h(c):
                def f():
                    dve.wait_ge(final_landed, 16)
                    for t in range(CHUNKS):
                        apply_gain(c, t)
                return f

            def apply_gain(c, t):
                dve.wait_ge(d_summed, 2 * c + t + 1)
                nc.vector.tensor_tensor(y_out[:, t, c * COLS:(c + 1) * COLS], h_tok[:, t, c * COLS:(c + 1) * COLS],
                                        final_b[:, c * COLS:(c + 1) * COLS], ALU.mult).then_inc(d_gained, 1)

            stream(N_DN, 2 * NP_F, both(f_last(BLK_F - 1), {NP_F + 2: [sum_down(0)], NP_F + 4: [gain_h(0)]}))
            stream(N_DN + 2 * NP_F, 2 * NP_F, {2: [sum_down(1)], 4: [gain_h(1)],
                                               NP_F + 2: [sum_down(2)], NP_F + 4: [gain_h(2)]})
            for t in range(CHUNKS):
                dve.wait_ge(d_last, t + 1)
                add_down(BLK_D - 1, t)
                apply_gain(BLK_D - 1, t)
                mean_square(d_sq, 2 * (BLK_D - 1) + t + 1, t + 1, t, t + 1)
                reciprocal_root(t + 1, t, t + 1)
                dve.wait_ge(h_rstd, t + 2)
                dve.wait_ge(d_gained, 2 * (BLK_D - 1) + t + 1)
                nc.vector.tensor_scalar(y_out[:, t, 0:DVE_COLS], y_out[:, t, 0:DVE_COLS], row_rstd[:, t:t + 1], None,
                                        ALU.mult).then_inc(fin_ready[t], 1)

        @block.tensor
        def _(pe):
            def features(src, k0, bank, c, k_all):
                def f():
                    s = c % SLOTS
                    for m in range(TILES):
                        out_m = ps[:, bank + m // 2, (m % 2) * SEQ:(m % 2 + 1) * SEQ]
                        for kk in range(KP):
                            k = c * KP + kk - k0
                            hi_w = w_hi[s][:, kk, m * P:(m + 1) * P]
                            lo_w = w_lo[s][:, kk, m * P:(m + 1) * P]
                            nc.tensor.matmul(out_m, hi_w, src[:, k, 0, :], start=(k == 0 and m % 2 == 0), stop=False,
                                             skip_group_check=True)
                            nc.tensor.matmul(out_m, hi_w, src[:, k, 1, :], start=False, stop=False,
                                             skip_group_check=True)
                            last = nc.tensor.matmul(out_m, lo_w, src[:, k, 0, :], start=False, stop=(k == k_all - 1),
                                                    skip_group_check=True)
                    return last
                return f

            def tokens(src, k0, bank, c, k_all, tiles=range(CHUNKS)):
                def f():
                    s = c % SLOTS
                    for t in tiles:
                        out_t = ps[:, bank + t, :]
                        for kk in range(KP):
                            k = k0 + kk
                            hi_a = src[:, k, 0, t * P:(t + 1) * P]
                            lo_a = src[:, k, 1, t * P:(t + 1) * P]
                            nc.tensor.matmul(out_t, hi_a, w_hi[s][:, kk, :], start=(k == 0), stop=False)
                            nc.tensor.matmul(out_t, hi_a, w_lo[s][:, kk, :], start=False, stop=False)
                            last = nc.tensor.matmul(out_t, lo_a, w_hi[s][:, kk, :], start=False, stop=(k == k_all - 1))
                    return last
                return f

            def stream(n0, products, steps):
                for c, multiply in enumerate(products):
                    for f in steps.get(c, []):
                        f()
                    pe.wait_ge(weights_split, n0 + c + 1)
                    multiply().then_inc(weights_used, 1)

            def both(a, b):
                return {k: a.get(k, []) + b.get(k, []) for k in sorted(set(a) | set(b))}

            def feature_block(src, bank, pieces, c0=0):
                return [features(src, c0 * KP, bank, c0 + c, pieces * KP) for c in range(pieces)]

            def token_block(src, bank, pieces, c0=0):
                return [(lambda c=c: tokens(src, c * KP, bank, c0 + c, pieces * KP)()) for c in range(pieces)]

            def wait(s, v):
                return lambda: pe.wait_ge(s, v)

            pe.wait_ge(masks_ready, 3)
            for _ in range(WARM_UP):
                nc.tensor.transpose(ps[:, 7, 0:P], ident[:, :], ident[:, :])
            for c in range(CHUNKS):
                pe.wait_ge(nrm_scaled, c + 1)
                for b in range(KD // 2 if c else KD // 2 - 1):
                    if b == KD // 2 - 1:
                        pe.wait_ge(params_ready, 1)
                    for j in range(2):
                        for cc in ([c] if b < 7 else range(CHUNKS)):
                            t = 2 * b + j
                            last = nc.tensor.transpose(ps[:, b, j * SEQ + cc * P:j * SEQ + (cc + 1) * P],
                                                       x_nrm[:, cc, t * P:(t + 1) * P], ident[:, :])
                    if c == CHUNKS - 1:
                        last.then_inc(nrm_t, 1)
                if c == 0:
                    pe.wait_ge(rows_landed, 16 * len(parameter_loads))
                    for j in range(PC_TABLES):
                        n = min(P, PC_ALL - j * P)
                        last = nc.tensor.transpose(ps[:, 7, j * P:j * P + n], par_rows[0:n, j, :], ident[0:n, 0:n])
                    last.then_inc(params_t, 1)

            def project_dt():
                pe.wait_ge(dtw_ready, 1)
                for k in range(KD):
                    nc.tensor.matmul(ps[0:HEADS, 7, :], dtw_hi[:, k, :], normed[:, k, :, :].rearrange("p a t -> p (a t)"),
                                     start=(k == 0), stop=False)
                    last = nc.tensor.matmul(ps[0:HEADS, 7, 0:SEQ], dtw_lo[:, k, :], normed[:, k, 0, :],
                                            start=False, stop=(k == KD - 1))
                last.then_inc(dt_sums, 1)

            def transpose_dt():
                pe.wait_ge(dt_cols_kept, 1)
                for c in range(CHUNKS):
                    last = nc.tensor.transpose(ps[:, 6, c * HEADS:(c + 1) * HEADS], dt_cols[:, c * P:(c + 1) * P],
                                               ident[0:HEADS, 0:HEADS])
                last.then_inc(dt_raw, 1)

            def running_sums():
                pe.wait_ge(dt_step, 20)
                nc.tensor.matmul(ps[:, 7, 0:HEADS], after_f[:, :], loga[:, 0, :], start=True, stop=True)
                nc.tensor.matmul(ps[:, 7, HEADS:2 * HEADS], upto[:, :], loga[:, 1, :], start=True, stop=True)\
                    .then_inc(cs_ready, 1)

            def transpose_b(i):
                def f():
                    pe.wait_ge(conv_act, 2 * i + 1)
                    pe.wait_ge(*((cb_kept, 2) if i else (dt_step, 1)))
                    for m in range(TILES):
                        last = nc.tensor.transpose(ps[:, 6, m * P:(m + 1) * P], b_feat[:, m, 0:P], ident[:, :])
                    last.then_inc(b_t, 1)
                return f

            def multiply_cb(i):
                def f():
                    pe.wait_ge(conv_act, 2 * i + 2)
                    pe.wait_ge(b_kept, i + 1)
                    pe.wait_ge(decays_ready, 2)
                    for c in range(CHUNKS):
                        for m in range(TILES):
                            last = nc.tensor.matmul(ps[:, 6 + c, m * P:(m + 1) * P], b_feat[:, m, c * P:(c + 1) * P],
                                                    c_feat[:, m, c * P:(c + 1) * P], start=True, stop=True)
                    last.then_inc(cb_ready, 1)
                return f

            for i in range(2):
                steps = {15: [transpose_b(i)]}
                if i == 0:
                    steps |= {c: [wait(nrm_lo, max(4, 2 * c + 2))] for c in range(8)}
                    steps |= {8: [project_dt], 11: [transpose_dt]}
                else:
                    steps |= {0: [wait(acc_copied, 1)], 1: [running_sums], 9: [multiply_cb(0)], 8: [wait(acc_copied, 2)]}
                stream(N_BC + 2 * i * NP_D,
                       feature_block(normed, 0, NP_D) + feature_block(normed, 4, NP_D, NP_D), steps)

            def segment(g, b):
                def f():
                    pe.wait_ge(seg_in, 8 * g + 2 * b + 2)
                    if not (isinstance(g, int) and g == 0 and b < 2):
                        pe.wait_ge(seg_exp, 4 * g + b - 1)
                    else:
                        pe.wait_ge(after_ready, 1)
                    nc.tensor.matmul(ps[:, 2 + b % 2, :], after[:, :], seg_hi[:, :, :].rearrange("p h l -> p (h l)"),
                                     start=True, stop=False)
                    nc.tensor.matmul(ps[:, 2 + b % 2, :], after[:, :], seg_lo[:, :, :].rearrange("p h l -> p (h l)"),
                                     start=False, stop=True).then_inc(seg_ready, 1)
                return f

            def transpose_x(g):
                def f():
                    pe.wait_ge(conv_act, g + 5)
                    if isinstance(g, int) and g == 0:
                        pe.wait_ge(cb_kept, 4)
                    else:
                        pe.wait_ge(yz_lo, 4 * g)
                    for c in range(CHUNKS):
                        for m in range(TILES):
                            last = nc.tensor.transpose(ps[:, 6 + c, m * P:(m + 1) * P],
                                                       x_conv[:, m, c * P:(c + 1) * P], ident[:, :])
                        last.then_inc(x_t, 1)
                return f

            def own_products(c):
                for h in range(HEADS_G):
                    last = nc.tensor.matmul(ps[:, 7, h * HEAD_DIM:(h + 1) * HEAD_DIM], mix[:, 2 * c + h // 4, h % 4, :],
                                            xdt[:, c, h * HEAD_DIM:(h + 1) * HEAD_DIM], start=True, stop=True)
                return last

            def first_chunk(g):
                def f():
                    pe.wait_ge(xprep, 5 * g + 5)
                    pe.wait_ge(now_kept, 2 * g + 2)
                    pe.wait_ge(mix_ready, 4 * g + 2)
                    nc.tensor.matmul(ps[:, 6, :], b_now[:, :], xdec[:, :], start=True, stop=True)
                    own_products(0).then_inc(y_first, 1)
                return f

            def second_chunk(g):
                def f():
                    pe.wait_ge(state_kept, g + 1)
                    pe.wait_ge(y_sum, 6 * g + 1)
                    pe.wait_ge(mix_ready, 4 * g + 4)
                    nc.tensor.matmul(ps[:, 6, :], c_now[:, :], state_sb[:, :], start=True, stop=True)
                    own_products(1).then_inc(y_second, 1)
                return f

            def transpose_yz(g):
                def f():
                    pe.wait_ge(g_scaled, 2 * g + 2)
                    for b in range(2):
                        for j in range(2):
                            for c in range(CHUNKS):
                                m = 2 * b + j
                                last = nc.tensor.transpose(ps[:, 6 + b, j * SEQ + c * P:j * SEQ + (c + 1) * P],
                                                           y[:, c, m * P:(m + 1) * P], ident[:, :])
                        last.then_inc(yz_t, 1)
                return f

            def own_steps(g):
                steps = {s: [segment(g, b)] for b, s in enumerate((3, 6, 9, 11))}
                return both(steps, {0: [wait(acc_copied, 3 if isinstance(g, int) else g + 4)],
                                    15: [transpose_x(g)]})

            def last_steps(g):
                return {3: [first_chunk(g)], 6: [second_chunk(g)], 12: [transpose_yz(g)]}

            group_products = feature_block(normed, 0, NP_D) + token_block(normed, 4, NP_D, NP_D)
            stream(N_G, group_products, both(own_steps(0), {8: [wait(acc_copied, 4)], 10: [multiply_cb(1)]}))
            with pe.Fori(0, GROUPS - 1) as g:
                stream((N_G + 2 * NP_D) + g * (2 * NP_D), group_products,
                       both(both(last_steps(g), own_steps(g + 1)), {8: [wait(z_kept, g + 1)]}))

            def transpose_value(v, src, bank, ready, first, freed, done, steps_free=1):
                def f():
                    pe.wait_ge(ready, v + 1)
                    if not first:
                        pe.wait_ge(freed, steps_free * v)
                    for m in range(TILES):
                        for c in range(CHUNKS):
                            last = nc.tensor.transpose(
                                ps[:, bank + m // 2, (m % 2) * SEQ + c * P:(m % 2) * SEQ + (c + 1) * P],
                                src[:, c, m * P:(m + 1) * P], ident[:, :])
                    last.then_inc(done, 1)
                return f

            os_products = token_block(normed, 0, NP_D) + token_block(yz, 2, NP_I, NP_D)
            stream(N_OS, os_products,
                   both(last_steps(GROUPS - 1),
                        {0: [wait(acc_copied, 4 + GROUPS)],
                         8: [wait(seg_exp, 4 * GROUPS)],
                         NP_D + NP_I - KP: [wait(yz_lo, 4 * GROUPS)]}))
            with pe.Fori(0, BLK_D - 1) as i:
                stream((N_OS + NP_D + NP_I) + i * (NP_D + NP_I), os_products,
                       {0: [wait(gate_done, i + 1)], 8: [wait(mb_done, i + 1)]})

            def transpose_ch(i, first=False):
                def f():
                    if not first:
                        pe.wait_ge(a_done, i)
                    transpose_value(i, a_tok, 6, ch_done, True, None, ch_t)()
                return f

            def transpose_b_part(i):
                def f():
                    pe.wait_ge(a_pre_kept, i + 1)
                    transpose_value(i, a_tok, 6, b_tok_kept, True, None, a_b_t)()
                return f

            a_products = (token_block(normed, 0, NP_D) + token_block(normed, 2, NP_D, NP_D)
                          + token_block(normed, 4, NP_D, 2 * NP_D))
            stream(N_A, a_products, {0: [wait(gate_done, BLK_D)], 8: [wait(mb_done, BLK_D)],
                                     16: [wait(z_kept, GROUPS)], 20: [wait(yz_lo, 4 * GROUPS), transpose_ch(0, True)]})
            with pe.Fori(0, BLK_D - 1) as i:
                stream((N_A + 3 * NP_D) + i * (3 * NP_D), a_products,
                       {0: [wait(ac_kept, i + 1)], 4: [transpose_b_part(i)], 8: [wait(ch_done, i + 1)],
                        16: [wait(b_tok_kept, i + 1)], 20: [transpose_ch(i + 1)]})

            oa_products = token_block(normed, 0, NP_D) + token_block(ya, 2, NP_D, NP_D)

            def transpose_out(v, first=False):
                return transpose_value(v, val, 4, val_done, first, out_lo, val_t)

            stream(N_OA, oa_products, {0: [wait(ac_kept, BLK_D)], 4: [transpose_b_part(BLK_D - 1)],
                                       8: [wait(ch_done, BLK_D)], 14: [wait(a_lo, BLK_D)]})
            stream(N_OA + 2 * NP_D, oa_products, {0: [wait(gate_done, BLK_D + 1)],
                                                  3: [wait(b_tok_kept, BLK_D), transpose_out(0, True)],
                                                  8: [wait(val_part, 1)]})
            with pe.Fori(0, BLK_D - 2) as i:
                stream((N_OA + 4 * NP_D) + i * (2 * NP_D), oa_products,
                       {0: [wait(gate_done, i + (BLK_D + 2))], 3: [transpose_out(i + 1)], 8: [wait(val_part, i + 2)]})

            def transpose_h(c):
                def f():
                    pe.wait_ge(h_sum, 2 * c + 2)
                    if c:
                        pe.wait_ge(h_lo, 4 * c)
                    for b in range(2):
                        for j in range(2):
                            for t in range(CHUNKS):
                                col = c * COLS + (2 * b + j) * P
                                last = nc.tensor.transpose(ps[:, 6 + b, j * SEQ + t * P:j * SEQ + (t + 1) * P],
                                                           h_tok[:, t, col:col + P], ident[:, :])
                        last.then_inc(h_t, 1)
                return f

            for c in range(BLK_D):
                steps = ({0: [wait(gate_done, 2 * BLK_D)], 3: [transpose_out(BLK_D - 1)], 6: [wait(out_lo, BLK_D)]},
                         {0: [wait(val_part, BLK_D)], 3: [transpose_h(0)]},
                         {3: [transpose_h(1)]},
                         {0: [wait(h_sum, 4)], 3: [transpose_h(2)]})[c]
                stream(N_O + c * NP_D, token_block(merged, 2 * (c % 2), NP_D), steps)

            f_products = token_block(normed, 0, NP_D) + token_block(normed, 2, NP_D, NP_D)
            stream(N_F, f_products, {0: [wait(h_sum, 6), wait(h_lo, 12)], 3: [transpose_h(3)], 6: [wait(h_lo, 16)]})
            with pe.Fori(0, BLK_F - 1) as i:
                stream((N_F + 2 * NP_D) + i * (2 * NP_D), f_products,
                       {0: [wait(gate_done, i + (2 * BLK_D + 1))], 3: [transpose_out(i + BLK_D)],
                        8: [wait(val_done, i + (BLK_D + 1))]})

            n_val = BLK_D + BLK_F
            for i in range(BLK_D // 2):
                products = token_block(ff, 0, NP_F) + token_block(ff, 2, NP_F, NP_F)
                if i == 0:
                    steps = {0: [wait(gate_done, BLK_D + n_val)], 3: [transpose_out(n_val - 1)],
                             NP_F - 2: [wait(out_lo, n_val)]}
                else:
                    steps = {0: [wait(d_summed, 2)], NP_F: [wait(d_summed, 4)]}
                tail = 0 if i == 0 else SLOTS
                stream(N_DN + i * 2 * NP_F, products[:2 * NP_F - tail], steps)
            for t in range(CHUNKS):
                for c in range(2 * NP_F - SLOTS, 2 * NP_F):
                    pe.wait_ge(weights_split, N_END - 2 * NP_F + c + 1)
                    last = tokens(ff, (c - NP_F) * KP, 2, c, KF, tiles=[t])()
                last.then_inc(d_last, 1)


_INS = ["x", "norm_mix_g", "w_in", "conv_a_w", "w_out_a", "ssm_conv_w", "ssm_conv_b", "dt_bias", "a_log", "d_skip",
        "ssm_norm_g", "w_out_ssm", "w_o", "norm_ffn_g", "w_ffn_gate", "w_ffn_up", "w_ffn_down", "norm_final_g"]
_OUTS = [((1, SEQ, D_MODEL), "float32")]


def kernel(**inputs):
    import numpy as _np
    import concourse.bacc as _bacc
    from concourse import mybir as _mybir
    from concourse.bass_utils import run_bass_kernel_spmd as _run

    nc = _bacc.Bacc("TRN2", target_bir_lowering=False, num_devices=1)
    arrays, args = {}, []
    for name in _INS:
        a = _np.ascontiguousarray(inputs[name])
        arrays[f"in_{name}_dram"] = a
        args.append(nc.dram_tensor(f"in_{name}_dram", a.shape, _mybir.dt.from_np(a.dtype), kind="ExternalInput").ap())
    for i, (shape, dtype) in enumerate(_OUTS):
        dt = _mybir.dt.from_np(_np.dtype(dtype))
        args.append(nc.dram_tensor(f"out_{i}_dram", shape, dt, kind="ExternalOutput").ap())
    hybrid_block_kernel(nc, *args)
    r = _run(nc, [arrays], core_ids=[0])
    return r.results[0]["out_0_dram"]
```
